# Optimizing a Trainium2 kernel written in Bass

```python
import jax
import jax.numpy as jnp
from jax import lax
import numpy as np

D_MODEL = 1024
BATCH = 1
SEQ = 512
DEPTH = 2

N_MIXERS = 4
MIXER_ORDER = ('stick_breaking', 'conformer_conv', 'dsa_sparse', 'mla')
Q_BLOCK = 128
CAUSAL_SEGMENTS = 16
ROPE_THETA = 10000.0
LN_EPS = 1e-5
RMS_EPS = 1e-6
DEEPNORM_ALPHA = (2.0 * DEPTH) ** 0.25
DEEPNORM_BETA = (8.0 * DEPTH) ** -0.25

MIX_WIDTH = D_MODEL
SB_HEADS = 8
SB_HEAD_DIM = MIX_WIDTH // SB_HEADS
CONV_CH = MIX_WIDTH
CONV_WIDTH = 31
DSA_HEADS = 16
DSA_HEAD_DIM = MIX_WIDTH // DSA_HEADS
IDX_HEADS = 8
IDX_DIM = 64
IDX_TOPK_MAX = 256
MLA_HEADS = 8
MLA_Q_RANK = 384
MLA_KV_RANK = 256
MLA_NOPE = 64
MLA_ROPE = 32
MLA_V = MIX_WIDTH // MLA_HEADS
MEM_TOKENS = 256
MEM_HEADS = 4
MEM_HEAD_DIM = 64
MEM_WIDTH = MEM_HEADS * MEM_HEAD_DIM
OUT_WIDTH = MIX_WIDTH + MEM_WIDTH
N_EXPERTS = 16
N_GROUPS = 4
EXPERTS_PER_GROUP = N_EXPERTS // N_GROUPS
TOPK_GROUPS = 1
TOPK_EXPERTS = 2
EXPERT_FF = 512
MOE_CHUNK = 512

W_IN_SB = 3 * MIX_WIDTH + MEM_WIDTH
W_IN_CONV = 2 * CONV_CH + MEM_WIDTH
W_IN_DSA = MIX_WIDTH + 2 * DSA_HEAD_DIM + IDX_HEADS * IDX_DIM + IDX_DIM + IDX_HEADS + MEM_WIDTH
W_IN_MLA = MLA_Q_RANK + MLA_KV_RANK + MLA_ROPE + MEM_WIDTH

F32 = jnp.float32

kernel_name = 'hybrid_stickbreak_conv_dsa_mla_sharedrouter_moe'

def _split_cols(h, sizes):
    idx = np.cumsum(sizes)[:-1].tolist()
    return jnp.split(h, idx, axis=-1)

def _layer_norm(x, g, b):
    xf = x.astype(F32)
    mu = jnp.mean(xf, axis=-1, keepdims=True)
    var = jnp.mean(jnp.square(xf - mu), axis=-1, keepdims=True)
    y = (xf - mu) * lax.rsqrt(var + LN_EPS) * g.astype(F32) + b.astype(F32)
    return y.astype(x.dtype)

def _rms_norm(x, g):
    xf = x.astype(F32)
    y = xf * lax.rsqrt(jnp.mean(jnp.square(xf), axis=-1, keepdims=True) + RMS_EPS) * g.astype(F32)
    return y.astype(x.dtype)

def _rope(x, pos):
    half = x.shape[-1] // 2
    inv_freq = ROPE_THETA ** (-jnp.arange(half, dtype=F32) / half)
    ang = pos.astype(F32)[..., None] * inv_freq
    cos = jnp.cos(ang)[:, :, None, :]
    sin = jnp.sin(ang)[:, :, None, :]
    xf = x.astype(F32)
    x1, x2 = xf[..., :half], xf[..., half:]
    return jnp.concatenate([x1 * cos - x2 * sin, x2 * cos + x1 * sin], axis=-1).astype(x.dtype)

def _to_blocks(a):
    a = a.reshape(a.shape[0], a.shape[1] // Q_BLOCK, Q_BLOCK, *a.shape[2:])
    return jnp.moveaxis(a, 1, 0)

def _from_blocks(a):
    a = jnp.moveaxis(a, 0, 1)
    return a.reshape(a.shape[0], a.shape[1] * a.shape[2], *a.shape[3:])

def _causal_sweep(block_fn, q_inputs, kv_inputs):
    seq = q_inputs[0].shape[1]
    n_blk = seq // Q_BLOCK
    n_seg = min(CAUSAL_SEGMENTS, n_blk)
    outs = []
    for j in range(n_seg):
        b0 = j * n_blk // n_seg
        b1 = (j + 1) * n_blk // n_seg
        k_len = b1 * Q_BLOCK
        kv = tuple(a[:, :k_len] for a in kv_inputs)
        qs = tuple(_to_blocks(a[:, b0 * Q_BLOCK:k_len]) for a in q_inputs)

        def body(args, kv=kv):
            return block_fn(*args, *kv)

        outs.append(_from_blocks(lax.map(body, (*qs, jnp.arange(b0, b1)))))
    return jnp.concatenate(outs, axis=1)

def _stick_breaking_attention(q, k, v):
    scale = q.shape[-1] ** -0.5

    def block(qb, blk, kf, vf):
        q_pos = blk * Q_BLOCK + jnp.arange(Q_BLOCK)
        key_pos = jnp.arange(kf.shape[1])
        z = jnp.einsum('bqhd,bkhd->bhqk', qb.astype(F32), kf.astype(F32)) * scale
        valid = key_pos[None, :] < q_pos[:, None]
        log_keep = jnp.where(valid, jax.nn.log_sigmoid(-z), 0.0)
        a = jnp.where(valid, jnp.exp(z + lax.cumsum(log_keep, axis=3, reverse=True)), 0.0)
        return jnp.einsum('bhqk,bkhd->bqhd', a, vf.astype(F32))

    return _causal_sweep(block, (q,), (k, v)).astype(v.dtype)

def _conformer_conv(a, g, conv_w, conv_b, norm_g, norm_b):
    h = a * jax.nn.sigmoid(g)
    hp = jnp.pad(h, ((0, 0), (CONV_WIDTH - 1, 0), (0, 0)))
    y = lax.conv_general_dilated(hp, conv_w[:, None, :].astype(h.dtype), window_strides=(1,), padding='VALID',
                                 dimension_numbers=('NWC', 'WIO', 'NWC'), feature_group_count=CONV_CH)
    y = y + conv_b.astype(y.dtype)
    return jax.nn.silu(_layer_norm(y, norm_g, norm_b))

def _dsa_attention(q, k, v, q_idx, k_idx, w_idx):
    seq = q.shape[1]
    n_sel_full = min(IDX_TOPK_MAX, seq // 4)
    scale = q.shape[-1] ** -0.5
    gather = jax.vmap(lambda src, ids: src[ids])

    def block(qb, qib, wb, blk, kk, vv, ki):
        k_len = kk.shape[1]
        n_sel = min(n_sel_full, k_len)
        q_pos = blk * Q_BLOCK + jnp.arange(Q_BLOCK)
        key_pos = jnp.arange(k_len)
        dots = jnp.einsum('bqhd,bkd->bqhk', qib.astype(F32), ki.astype(F32)) * (IDX_DIM ** -0.5)
        score = jnp.einsum('bqh,bqhk->bqk', wb.astype(F32) * (IDX_HEADS ** -0.5), jax.nn.relu(dots))
        score = jnp.where((key_pos[None, :] <= q_pos[:, None])[None], score, -jnp.inf)
        _, sel = lax.top_k(score, n_sel)
        sel_ok = sel <= q_pos[None, :, None]
        kg = gather(kk, sel).astype(F32)
        vg = gather(vv, sel).astype(F32)
        s = jnp.einsum('bqhd,bqkd->bhqk', qb.astype(F32), kg) * scale
        s = jnp.where(sel_ok[:, None], s, -jnp.inf)
        p = jax.nn.softmax(s, axis=-1)
        return jnp.einsum('bhqk,bqkd->bqhd', p, vg)

    return _causal_sweep(block, (q, q_idx, w_idx), (k, v, k_idx)).astype(v.dtype)

def _mla_attention(c_q, c_kv, k_rope, pos, q_norm_g, kv_norm_g, w_q_up, w_kv_up):
    bsz, seq = c_q.shape[:2]
    q = (_rms_norm(c_q, q_norm_g) @ w_q_up).reshape(bsz, seq, MLA_HEADS, MLA_NOPE + MLA_ROPE)
    q_nope, q_rope = q[..., :MLA_NOPE], _rope(q[..., MLA_NOPE:], pos)
    kv = (_rms_norm(c_kv, kv_norm_g) @ w_kv_up).reshape(bsz, seq, MLA_HEADS, MLA_NOPE + MLA_V)
    k_nope, v = kv[..., :MLA_NOPE], kv[..., MLA_NOPE:]
    kr = _rope(k_rope[:, :, None, :], pos)[:, :, 0]
    scale = (MLA_NOPE + MLA_ROPE) ** -0.5

    def block(qn, qr, blk, kn, krr, vf):
        q_pos = blk * Q_BLOCK + jnp.arange(Q_BLOCK)
        key_pos = jnp.arange(kn.shape[1])
        s = (jnp.einsum('bqhd,bkhd->bhqk', qn.astype(F32), kn.astype(F32))
             + jnp.einsum('bqhd,bkd->bhqk', qr.astype(F32), krr.astype(F32))) * scale
        s = jnp.where(key_pos[None, :] <= q_pos[:, None], s, -jnp.inf)
        p = jax.nn.softmax(s, axis=-1)
        return jnp.einsum('bhqk,bkhd->bqhd', p, vf.astype(F32))

    out = _causal_sweep(block, (q_nope, q_rope), (k_nope, kr, v))
    return out.reshape(bsz, seq, MLA_HEADS * MLA_V).astype(c_q.dtype)

def _memory_attention(mq, mem, w_mem_kv):
    bsz, seq = mq.shape[:2]
    q = mq.reshape(bsz, seq, MEM_HEADS, MEM_HEAD_DIM).astype(F32)
    kv = (mem @ w_mem_kv).reshape(bsz, mem.shape[1], 2, MEM_HEADS, MEM_HEAD_DIM).astype(F32)
    s = jnp.einsum('bqhd,bmhd->bhqm', q, kv[:, :, 0]) * (MEM_HEAD_DIM ** -0.5)
    p = jax.nn.softmax(s, axis=-1)
    out = jnp.einsum('bhqm,bmhd->bqhd', p, kv[:, :, 1])
    return out.reshape(bsz, seq, MEM_WIDTH).astype(mq.dtype)

def _moe_ffn(x, router_w, router_bias, w_in, w_out):
    bsz, seq, d = x.shape
    t = x.reshape(bsz * seq, d)
    n_tok = t.shape[0]
    s = jax.nn.sigmoid(t.astype(F32) @ router_w.astype(F32))
    sb = s + router_bias.astype(F32)
    g_score = lax.top_k(sb.reshape(-1, N_GROUPS, EXPERTS_PER_GROUP), 2)[0].sum(-1)
    _, g_sel = lax.top_k(g_score, TOPK_GROUPS)
    g_mask = jnp.any(g_sel[..., None] == jnp.arange(N_GROUPS), axis=1)
    e_mask = jnp.repeat(g_mask, EXPERTS_PER_GROUP, axis=1)
    _, e_sel = lax.top_k(jnp.where(e_mask, sb, -jnp.inf), TOPK_EXPERTS)
    gw = jnp.take_along_axis(s, e_sel, axis=1)
    gw = gw / jnp.sum(gw, axis=-1, keepdims=True)

    n_asg = n_tok * TOPK_EXPERTS
    n_chunks = -(-n_asg // MOE_CHUNK) + N_EXPERTS
    e_flat = e_sel.reshape(-1)
    order = jnp.argsort(e_flat)
    e_sorted = e_flat[order]
    tok_sorted = order // TOPK_EXPERTS
    w_sorted = gw.reshape(-1)[order]
    counts = jnp.bincount(e_flat, length=N_EXPERTS)
    padded = (counts + MOE_CHUNK - 1) // MOE_CHUNK * MOE_CHUNK
    pad_end = jnp.cumsum(padded)
    pad_start = pad_end - padded
    start = jnp.cumsum(counts) - counts
    slot = pad_start[e_sorted] + jnp.arange(n_asg) - start[e_sorted]
    buf = jnp.zeros((n_chunks * MOE_CHUNK, d), t.dtype).at[slot].set(t[tok_sorted])
    chunk_exp = jnp.clip(jnp.searchsorted(pad_end, jnp.arange(n_chunks) * MOE_CHUNK, side='right'),
                         0, N_EXPERTS - 1)
    xb = buf.reshape(n_chunks, MOE_CHUNK, d)
    h = jnp.einsum('ncd,ndf->ncf', xb, w_in[chunk_exp])
    h = jax.nn.silu(h[..., :EXPERT_FF]) * h[..., EXPERT_FF:]
    yb = jnp.einsum('ncf,nfd->ncd', h, w_out[chunk_exp]).reshape(-1, d)
    y_asg = yb[slot].astype(F32) * w_sorted[:, None]
    y = jax.ops.segment_sum(y_asg, tok_sorted, num_segments=n_tok)
    return y.reshape(bsz, seq, d).astype(x.dtype)

def setup_inputs(seed: int = 0) -> dict:
    key = jax.random.key(seed)
    keys = iter(jax.random.split(key, 64))

    def nrm(shape, scale):
        return jax.random.normal(next(keys), shape, F32) * scale

    def gain(shape):
        return 1.0 + nrm(shape, 0.02)

    def mem_wkv():
        w = nrm((D_MODEL, 2 * MEM_WIDTH), D_MODEL ** -0.5)
        return w.at[:, MEM_WIDTH:].multiply(DEEPNORM_BETA)

    def w_o():
        return nrm((OUT_WIDTH, D_MODEL), OUT_WIDTH ** -0.5 * DEEPNORM_BETA)

    def moe_in():
        return nrm((N_EXPERTS, D_MODEL, 2 * EXPERT_FF), D_MODEL ** -0.5)

    def moe_out():
        return nrm((N_EXPERTS, EXPERT_FF, D_MODEL), EXPERT_FF ** -0.5 * DEEPNORM_BETA)

    inp = {}
    inp['x'] = nrm((BATCH, SEQ, D_MODEL), 1.0)
    inp['mem'] = nrm((BATCH, MEM_TOKENS, D_MODEL), 1.0)
    inp['positions'] = (jax.random.randint(next(keys), (BATCH, 1), 0, 4096, dtype=jnp.int32)
                        + jnp.arange(SEQ, dtype=jnp.int32)[None, :])
    inp['router_w'] = nrm((D_MODEL, N_EXPERTS), D_MODEL ** -0.5)
    inp['router_bias'] = nrm((N_EXPERTS,), 0.01)
    inp['l0_w_in'] = nrm((D_MODEL, W_IN_SB), D_MODEL ** -0.5)
    inp['l0_mem_wkv'] = mem_wkv()
    inp['l0_w_o'] = w_o()
    inp['l0_ln_g'] = gain((2, D_MODEL))
    inp['l0_ln_b'] = nrm((2, D_MODEL), 0.02)
    inp['l0_moe_w_in'] = moe_in()
    inp['l0_moe_w_out'] = moe_out()
    inp['l1_w_in'] = nrm((D_MODEL, W_IN_CONV), D_MODEL ** -0.5)
    inp['l1_conv_w'] = nrm((CONV_WIDTH, CONV_CH), CONV_WIDTH ** -0.5)
    inp['l1_conv_b'] = nrm((CONV_CH,), 0.02)
    inp['l1_conv_norm_g'] = gain((CONV_CH,))
    inp['l1_conv_norm_b'] = nrm((CONV_CH,), 0.02)
    inp['l1_mem_wkv'] = mem_wkv()
    inp['l1_w_o'] = w_o()
    inp['l1_ln_g'] = gain((2, D_MODEL))
    inp['l1_ln_b'] = nrm((2, D_MODEL), 0.02)
    inp['l1_moe_w_in'] = moe_in()
    inp['l1_moe_w_out'] = moe_out()
    inp['l2_w_in'] = nrm((D_MODEL, W_IN_DSA), D_MODEL ** -0.5)
    inp['l2_mem_wkv'] = mem_wkv()
    inp['l2_w_o'] = w_o()
    inp['l2_ln_g'] = gain((2, D_MODEL))
    inp['l2_ln_b'] = nrm((2, D_MODEL), 0.02)
    inp['l2_moe_w_in'] = moe_in()
    inp['l2_moe_w_out'] = moe_out()
    inp['l3_w_in'] = nrm((D_MODEL, W_IN_MLA), D_MODEL ** -0.5)
    inp['l3_q_norm_g'] = gain((MLA_Q_RANK,))
    inp['l3_kv_norm_g'] = gain((MLA_KV_RANK,))
    inp['l3_w_q_up'] = nrm((MLA_Q_RANK, MLA_HEADS * (MLA_NOPE + MLA_ROPE)), MLA_Q_RANK ** -0.5)
    inp['l3_w_kv_up'] = nrm((MLA_KV_RANK, MLA_HEADS * (MLA_NOPE + MLA_V)), MLA_KV_RANK ** -0.5)
    inp['l3_mem_wkv'] = mem_wkv()
    inp['l3_w_o'] = w_o()
    inp['l3_ln_g'] = gain((2, D_MODEL))
    inp['l3_ln_b'] = nrm((2, D_MODEL), 0.02)
    inp['l3_moe_w_in'] = moe_in()
    inp['l3_moe_w_out'] = moe_out()
    return inp

def reference(x, mem, positions, router_w, router_bias,
              l0_w_in, l0_mem_wkv, l0_w_o, l0_ln_g, l0_ln_b, l0_moe_w_in, l0_moe_w_out,
              l1_w_in, l1_conv_w, l1_conv_b, l1_conv_norm_g, l1_conv_norm_b, l1_mem_wkv, l1_w_o,
              l1_ln_g, l1_ln_b, l1_moe_w_in, l1_moe_w_out,
              l2_w_in, l2_mem_wkv, l2_w_o, l2_ln_g, l2_ln_b, l2_moe_w_in, l2_moe_w_out,
              l3_w_in, l3_q_norm_g, l3_kv_norm_g, l3_w_q_up, l3_w_kv_up, l3_mem_wkv, l3_w_o,
              l3_ln_g, l3_ln_b, l3_moe_w_in, l3_moe_w_out):
    layers = [
        dict(w_in=l0_w_in, mem_wkv=l0_mem_wkv, w_o=l0_w_o, ln_g=l0_ln_g, ln_b=l0_ln_b,
             moe_w_in=l0_moe_w_in, moe_w_out=l0_moe_w_out),
        dict(w_in=l1_w_in, mem_wkv=l1_mem_wkv, w_o=l1_w_o, ln_g=l1_ln_g, ln_b=l1_ln_b,
             moe_w_in=l1_moe_w_in, moe_w_out=l1_moe_w_out, conv_w=l1_conv_w, conv_b=l1_conv_b,
             conv_norm_g=l1_conv_norm_g, conv_norm_b=l1_conv_norm_b),
        dict(w_in=l2_w_in, mem_wkv=l2_mem_wkv, w_o=l2_w_o, ln_g=l2_ln_g, ln_b=l2_ln_b,
             moe_w_in=l2_moe_w_in, moe_w_out=l2_moe_w_out),
        dict(w_in=l3_w_in, mem_wkv=l3_mem_wkv, w_o=l3_w_o, ln_g=l3_ln_g, ln_b=l3_ln_b,
             moe_w_in=l3_moe_w_in, moe_w_out=l3_moe_w_out, q_norm_g=l3_q_norm_g,
             kv_norm_g=l3_kv_norm_g, w_q_up=l3_w_q_up, w_kv_up=l3_w_kv_up),
    ]
    bsz, seq, _ = x.shape
    for i in range(DEPTH):
        p = layers[i]
        kind = MIXER_ORDER[i % N_MIXERS]
        h = x @ p['w_in']
        if kind == 'stick_breaking':
            q, k, v, mq = _split_cols(h, [MIX_WIDTH, MIX_WIDTH, MIX_WIDTH, MEM_WIDTH])
            shp = (bsz, seq, SB_HEADS, SB_HEAD_DIM)
            mix = _stick_breaking_attention(q.reshape(shp), k.reshape(shp), v.reshape(shp))
            mix = mix.reshape(bsz, seq, MIX_WIDTH)
        elif kind == 'conformer_conv':
            a, g, mq = _split_cols(h, [CONV_CH, CONV_CH, MEM_WIDTH])
            mix = _conformer_conv(a, g, p['conv_w'], p['conv_b'], p['conv_norm_g'], p['conv_norm_b'])
        elif kind == 'dsa_sparse':
            q, k, v, qi, ki, wi, mq = _split_cols(
                h, [MIX_WIDTH, DSA_HEAD_DIM, DSA_HEAD_DIM, IDX_HEADS * IDX_DIM, IDX_DIM, IDX_HEADS, MEM_WIDTH])
            q = _rope(q.reshape(bsz, seq, DSA_HEADS, DSA_HEAD_DIM), positions)
            k = _rope(k[:, :, None, :], positions)[:, :, 0]
            qi = _rope(qi.reshape(bsz, seq, IDX_HEADS, IDX_DIM), positions)
            ki = _rope(ki[:, :, None, :], positions)[:, :, 0]
            mix = _dsa_attention(q, k, v, qi, ki, wi).reshape(bsz, seq, MIX_WIDTH)
        else:
            c_q, c_kv, k_rope, mq = _split_cols(h, [MLA_Q_RANK, MLA_KV_RANK, MLA_ROPE, MEM_WIDTH])
            mix = _mla_attention(c_q, c_kv, k_rope, positions, p['q_norm_g'], p['kv_norm_g'],
                                 p['w_q_up'], p['w_kv_up'])
        mem_out = _memory_attention(mq, mem, p['mem_wkv'])
        y = jnp.concatenate([mix, mem_out], axis=-1) @ p['w_o']
        x = _layer_norm(DEEPNORM_ALPHA * x + y, p['ln_g'][0], p['ln_b'][0])
        f = _moe_ffn(x, router_w, router_bias, p['moe_w_in'], p['moe_w_out'])
        x = _layer_norm(DEEPNORM_ALPHA * x + f, p['ln_g'][1], p['ln_b'][1])
    return x


_drawn_inputs = setup_inputs


def setup_inputs(seed=0):
    import zlib

    import numpy as np

    out = dict(_drawn_inputs(seed))
    spreads = {}
    factors = {'l1_conv_b': 4.357, 'l1_conv_norm_g': 5.775, 'l1_conv_norm_b': 6.064, 'l1_mem_wkv': 4.691}
    for name, (base, spread) in spreads.items():
        noise = np.random.default_rng([zlib.crc32(name.encode()), seed]).standard_normal(out[name].shape)
        drawn = base * np.exp(spread * noise) if base else spread * noise
        out[name] = jnp.asarray(drawn.astype(out[name].dtype))
    for name, factor in factors.items():
        out[name] = (out[name] * factor).astype(out[name].dtype)
    return out
```

```python
from contextlib import ExitStack

import concourse.bass as bass
from concourse import mybir

ALU = mybir.AluOpType
ACT = mybir.ActivationFunctionType
AX_X = mybir.AxisListType.X
F32 = mybir.dt.float32
I32 = mybir.dt.int32

P = 128
S, D = 512, 1024
TT, KD = S // P, D // P
MEM = 256
MT = MEM // P
HEADS = 8
MEM_HEADS, MEM_DH = 4, 64
MIX_TILES = D // P + MEM_HEADS * MEM_DH // P
TAPS = 31
PE_TAPS = 4
E, GROUPS, PER_GROUP, FF = 16, 4, 4, 512
FK = FF // P
ALPHA = (2.0 * 2) ** 0.25
LN_EPS = 1e-5
BIG = 1e30

SLOTS = 6
COLS = 256
PIECE = 2
CA = KD // PIECE
CB = FK // PIECE
CW = MIX_TILES // PIECE
N_KV = 4
N_IN = (1 + 3 * 4, 9)
STEP = CA + CB
BASE_IN = (N_KV, N_KV + N_IN[0] + CW + E * STEP)
BASE_WO = (BASE_IN[0] + N_IN[0], BASE_IN[1] + N_IN[1])
BASE_MOE = (BASE_WO[0] + CW, BASE_WO[1] + CW)

CAP = 128
ROUNDS = S // CAP


FAR_DVE = 5 * (ROUNDS - 1) * E + 1


def slot_of(n):
    return n % SLOTS


def loaded(n):
    return 16 * (n // SLOTS + 1)


def first_done(base, e):
    return base + CA if isinstance(e, int) and e == 0 else base + 2 * CA - STEP + STEP * e


def second_done(base, e):
    return base + E * STEP if isinstance(e, int) and e == E - 1 else STEP * e + (base + CA + STEP)


class Order:

    def __init__(self, engine, semaphore):
        self.engine, self.semaphore, self.n = engine, semaphore, 0

    def mark(self, instruction):
        instruction.then_inc(self.semaphore, 1)
        self.n = self.n + 1

    def wait(self):
        self.engine.wait_ge(self.semaphore, self.n)


def build(nc, x, mem, router_w, router_bias,
          l0_w_in, l0_mem_wkv, l0_w_o, l0_ln_g, l0_ln_b, l0_moe_w_in, l0_moe_w_out,
          l1_w_in, l1_conv_w, l1_conv_b, l1_conv_norm_g, l1_conv_norm_b, l1_mem_wkv, l1_w_o,
          l1_ln_g, l1_ln_b, l1_moe_w_in, l1_moe_w_out, out):
    w_in, mem_wkv, w_o = (l0_w_in, l1_w_in), (l0_mem_wkv, l1_mem_wkv), (l0_w_o, l1_w_o)
    ln_g, ln_b = (l0_ln_g, l1_ln_g), (l0_ln_b, l1_ln_b)
    moe_in, moe_out = (l0_moe_w_in, l1_moe_w_in), (l0_moe_w_out, l1_moe_w_out)

    rows_dram = [nc.dram_tensor(f"rows{i}", [S, D], F32, kind="Internal").ap() for i in range(2)]
    near_dram = [nc.dram_tensor(f"near{i}", [E * CAP, D], F32, kind="Internal").ap() for i in range(2)]
    far_dram = nc.dram_tensor("far", [E * S, D], F32, kind="Internal").ap()
    token_of_slot = [nc.dram_tensor(f"token_of_slot{i}", [E * S, 1], I32, kind="Internal").ap() for i in range(2)]

    with ExitStack() as ctx:
        def sb(name, shape, dt=F32):
            return ctx.enter_context(nc.sbuf_tensor(name, shape, dt))

        def sem(name):
            return ctx.enter_context(nc.semaphore(name))

        def two(name):
            return [sem(f"{name}{i}") for i in range(2)]

        ps = ctx.enter_context(nc.psum_tensor("ps", [P, 8, 512], F32))

        xrow = sb("xrow", [P, TT, D])
        xT = sb("xT", [P, KD, S])
        mixT = sb("mixT", [P, MIX_TILES, S])
        ring = sb("ring", [P, SLOTS, 2048])
        mqT = sb("mqT", [P, 2, S])
        kTm = sb("kTm", [P, 2, 2, MEM])
        vm = sb("vm", [P, 2, MT, MEM])
        lnp = sb("lnp", [P, 2, D])
        ident = sb("ident", [P, P])
        neg_tri = sb("neg_tri", [P, P])
        neg_one = sb("neg_one", [P, P])
        before = sb("before", [P, P])
        ones = sb("ones", [P, P])
        rw = sb("rw", [P, KD, E])
        rb = sb("rb", [P, TT, E])
        tok_id = sb("tok_id", [P, TT], I32)
        seg_base = sb("seg_base", [P, TT, E])
        rank_e = sb("rank_e", [P, TT, E])
        rank_g = sb("rank_g", [P, TT, GROUPS])
        minus_half = sb("minus_half", [P, 1])
        zero_tab = sb("zero_tab", [P, E * S // P], I32)
        stats = sb("stats", [P, TT, 2, 6])
        mv = sb("mv", [P, TT, 2])
        rstd = sb("rstd", [P, TT])
        lt = sb("lt", [P, 2, S])
        probs, pT = sb("probs", [P, TT, MEM]), sb("pT", [P, MT, S])
        mstat = sb("mstat", [P, 2, TT])

        sc = sb("sc", [P, TT, E])
        scb = sb("scb", [P, TT, E])
        pair = sb("pair", [P, TT * GROUPS, 6])
        gs = sb("gs", [P, TT, GROUPS])
        ge = sb("ge", [P, TT, GROUPS])
        top = sb("top", [P, TT])
        ekey = sb("ekey", [P, TT, E])
        oh1 = sb("oh1", [P, TT, E])
        oh2 = sb("oh2", [P, TT, E])
        both = sb("both", [P, TT, E])
        gate = sb("gate", [P, 2, TT])
        gsum = sb("gsum", [P, TT])
        slot_f = sb("slot_f", [P, 2, TT])
        slot_i = sb("slot_i", [P, 2, TT], I32)
        near_base = sb("near_base", [P, TT, E])
        over = sb("over", [P, TT, E])
        near_f, near_gate, far_gate = sb("near_f", [P, 2, TT]), sb("near_gate", [P, 2, TT]), sb("far_gate", [P, 2, TT])
        near_i = sb("near_i", [P, 2, TT], I32)
        most_f = sb("most_f", [P, 1])
        most = sb("most", [P, 1], I32)
        tab_i = sb("tab_i", [E * ROUNDS, CAP], I32)
        tab_f = sb("tab_f", [E * ROUNDS, CAP])
        slot_tok = sb("slot_tok", [P, E * ROUNDS], I32)

        arena = sb("arena", [P, 8960])

        def part(start, *shape):
            size = 1
            for n in shape:
                size *= n
            flat = arena[:, start:start + size]
            if len(shape) == 1:
                return flat
            names = "abc"[:len(shape)]
            return flat.rearrange(f"p ({' '.join(names)}) -> p {' '.join(names)}", **dict(zip(names, shape)))

        memrow, memT = part(0, MT, D), part(2048, KD, MEM)
        qT, kT, v = part(0, 4, S), part(2048, 4, S), part(4096, 8, COLS)
        soft, aT = part(6144, 1280), part(7424, 1280)
        HP = S + 32
        hpad = part(0, KD, HP)
        cv = KD * HP
        dg = part(cv, 2 * PE_TAPS, P)
        gl = part(cv + 2 * PE_TAPS * P, 2, S)
        mean_b, rs_b, t0, t1 = (part(cv + 2 * PE_TAPS * P + 2 * S + i * S, S) for i in range(4))
        xg, xgT = part(0, 2, D), part(2048, 2, KD, CAP)
        hact, hT, yo = part(4096, 2, FF), part(5120, 2, FK, CAP), part(6144, 2, D)
        yg = part(0, 2 * TT, D)
        mem_bank = (0, 4)
        conv_rows = sb("conv_rows", [TAPS + 3, D])
        convc = sb("convc", [P, KD, TAPS + 3])

        landed = [sem(f"landed{i}") for i in range(SLOTS)]
        chunks_used = sem("chunks_used")
        x_in, mem_in, small_in, conv_in, tab_in = sem("x_in"), sem("mem_in"), sem("small_in"), sem("conv_in"), sem("tab_in")
        ln_in = sem("ln_in")
        consts, consts2 = sem("consts"), sem("consts2")
        v_order, a_order, g_order = sem("v_order"), sem("a_order"), sem("g_order")
        tp_mm, xT_a, xT_v = sem("tp_mm"), sem("xT_a"), sem("xT_v")
        mt_mm, mt_a, mt_v = sem("mt_mm"), sem("mt_a"), sem("mt_v")
        kv_mm, kv_ev = sem("kv_mm"), sem("kv_ev")
        pj_mm, pj_ev = sem("pj_mm"), sem("pj_ev")
        z_mm, abs_v, e_a, l_a, soft_v, soft_g, c_mm, w_a, w_g, av_mm, av_ev = (
            sem(n) for n in ("z_mm", "abs_v", "e_a", "l_a", "soft_v", "soft_g", "c_mm", "w_a", "w_g", "av_mm", "av_ev"))
        ms_mm, ms_v, ms_a, mp_v, mt2_mm, mt2_v, mo_mm, mo_v = (
            sem(n) for n in ("ms_mm", "ms_v", "ms_a", "mp_v", "mt2_mm", "mt2_v", "mo_mm", "mo_v"))
        op_mm, op_v = sem("op_mm"), sem("op_v")
        ln_var, ln_rs, row_ready = sem("ln_var"), sem("ln_rs"), sem("row_ready")
        rows_out = sem("rows_out")
        rt_mm, sig_a, pick_v, pos_mm, slots_v, scat, tab_mm, slot_tok_v, tabf_v = (
            sem(n) for n in ("rt_mm", "sig_a", "pick_v", "pos_mm", "slots_v", "scat", "tab_mm", "slot_tok_v", "tabf_v"))
        tab_ld = sem("tab_ld")
        gat = two("gat")
        xt_mm, xt_a, xt_v, sg_a, sg_v, h_v, ht_mm, ht_v, y_a, y_v = (
            sem(n) for n in ("xt_mm", "xt_a", "xt_v", "sg_a", "sg_v", "h_v", "ht_mm", "ht_v", "y_a", "y_v"))
        y_st = two("y_st")
        o_clear, o_zero = two("o_clear"), two("o_zero")
        o_far = [two("o_far_l0_"), two("o_far_l1_")]
        o_w, o_x, o_pe, o_dve, o_sg, o_st = (two(n) for n in ("o_w", "o_x", "o_pe", "o_dve", "o_sg", "o_st"))
        yg_in = [sem(f"yg_in{k}") for k in range(2 * TT)]
        yg_v = sem("yg_v")
        pad_g = sem("pad_g")
        cc_mm, cc_v = sem("cc_mm"), sem("cc_v")
        mq_mm = two("mq_mm")
        gl_mm, gl_a, gl_v = sem("gl_mm"), sem("gl_a"), sem("gl_v")
        mq_v = sem("mq_v")
        dg_a, cv_mm, cv_a, cv_v = sem("dg_a"), sem("cv_mm"), sem("cv_a"), sem("cv_v")
        mu_mm, mu_v, yc_v, sq_a, var_mm, var_v, lnv_a, rsb_v, u_v, su_a, mix_v = (
            sem(n) for n in ("mu_mm", "mu_v", "yc_v", "sq_a", "var_mm", "var_v", "lnv_a", "rsb_v", "u_v", "su_a", "mix_v"))
        out_done = sem("out_done")

        block = ctx.enter_context(nc.Block())

        def kv_event(j):
            return (chunks_used, j // 2 + 1) if j % 2 else (kv_mm, j // 2 + 1)

        def mq_event(layer, j):
            return (chunks_used, BASE_IN[layer] + 1) if j else (mq_mm[layer], 1)

        def proj_event(g, i):
            first = BASE_IN[0] + 1 + 3 * g
            if i in (1, 3, 7):
                return chunks_used, first + {1: 1, 3: 2, 7: 3}[i]
            return pj_mm, 5 * g + {0: 1, 2: 2, 4: 3, 5: 4, 6: 5}[i]

        def gate_event(j):
            return (chunks_used, BASE_IN[1] + 1 + 2 * (j // 2 + 1)) if j % 2 else (gl_mm, j // 2 + 1)

        def out_event(layer, j):
            return (chunks_used, BASE_MOE[layer]) if j == 2 * TT - 1 else (op_mm, j + 1 + layer * (2 * TT - 1))

        def col_chunk(w, c0):
            return w[:, c0:c0 + COLS].rearrange("(k p) n -> p k n", p=P)

        def ring_cols(n):
            return ring[:, slot_of(n), :].rearrange("p (k n) -> p k n", n=COLS)

        def ring_rows(n):
            return ring[:, slot_of(n), :].rearrange("p (k n) -> p k n", n=D)

        def expert_rows(w, e, c):
            view = w.rearrange("e (c k p) n -> c e p k n", k=PIECE, p=P)[c]
            if isinstance(e, int):
                return view[e]
            return view[bass.ds(e, 1)].rearrange("e p k n -> p (e k) n")

        def blk(kb):
            start = sum((TT - j) * P for j in range(kb))
            return start, (TT - kb) * P

        @block.sync
        def _(sp):
            xt = x[0].rearrange("(t p) d -> p t d", p=P)
            for t in range(TT):
                sp.dma_start(xrow[:, t, :], xt[:, t, :]).then_inc(x_in, 16)
            sp.dma_start(memrow, mem[0].rearrange("(t p) d -> p t d", p=P)).then_inc(mem_in, 16)

            def load(n, dst, src):
                if n >= SLOTS:
                    sp.wait_ge(chunks_used, n - SLOTS + 1)
                sp.dma_start(dst, src).then_inc(landed[slot_of(n)], 16)

            for layer in range(2):
                for j in range(2):
                    load(2 * layer + j, ring_cols(2 * layer + j), col_chunk(mem_wkv[layer], j * COLS))
            sp.dma_start(rw[:, :, :], router_w.rearrange("(k p) e -> p k e", p=P)).then_inc(small_in, 16)
            for t in range(TT):
                sp.dma_start(rb[:, t, :], router_bias.partition_broadcast(P)).then_inc(small_in, 16)
            sp.dma_start(conv_rows[0:TAPS, :], l1_conv_w).then_inc(conv_in, 16)
            for i, row in enumerate((l1_conv_b, l1_conv_norm_g, l1_conv_norm_b)):
                sp.dma_start(conv_rows[TAPS + i:TAPS + i + 1, :], row.rearrange("(a n) -> a n", a=1)).then_inc(conv_in, 16)

            def load_ln(i):
                layer, which = i // 2, i % 2
                if i:
                    sp.wait_ge(row_ready, (i - 1) * TT + TT)
                sp.dma_start(lnp[:, 0, :], ln_g[layer][which].partition_broadcast(P)).then_inc(ln_in, 16)
                sp.dma_start(lnp[:, 1, :], ln_b[layer][which].partition_broadcast(P)).then_inc(ln_in, 16)

            load_ln(0)

            def moe_loads(layer):
                base = BASE_MOE[layer]
                for c in range(CA):
                    load(base + c, ring_rows(base + c), expert_rows(moe_in[layer], 0, c))
                for t in range(TT):
                    sp.wait_ge(row_ready, (2 * layer) * TT + t + 1)
                    sp.dma_start(rows_dram[layer][t * P:(t + 1) * P, :], xrow[:, t, :]).then_inc(rows_out, 16)
                load_ln(2 * layer + 1)

                def step(s, e_next, e_last):
                    for c in range(STEP):
                        n = base + CA + c
                        src = expert_rows(moe_in[layer], e_next, c) if c < CA else expert_rows(moe_out[layer], e_last, c - CA)
                        sp.wait_ge(chunks_used, s * STEP + (n - SLOTS + 1))
                        sp.dma_start(ring_rows(n), src).then_inc(landed[slot_of(n)], 16)

                with sp.Fori(0, E - 1) as s:
                    step(s, s + 1, s)
                n0 = base + E * STEP - CB
                for c in range(CB):
                    load(n0 + c, ring_rows(n0 + c), expert_rows(moe_out[layer], E - 1, c))

            def overflow(layer):
                sp.wait_ge(slots_v, 2 + layer * 2)
                most_reg = sp.value_load(most[0:1, 0:1], min_val=0, max_val=S)
                with sp.If(most_reg > CAP):
                    sp.wait_ge(chunks_used, BASE_MOE[layer] + E * STEP)
                    with sp.Fori(0, (ROUNDS - 1) * E) as i:
                        e = i % E
                        for c in range(STEP):
                            src = expert_rows(moe_in[layer], e, c) if c < CA else expert_rows(moe_out[layer], e, c - CA)
                            sp.wait_ge(o_pe[layer], 4 * i + 4)
                            sp.dma_start(ring_rows(c), src).then_inc(o_w[layer], 16)
                    sp.wait_ge(o_pe[layer], 4 * (ROUNDS - 1) * E + 4)

            load(BASE_IN[0], ring_cols(BASE_IN[0]), col_chunk(w_in[0], 3 * D))
            for g in range(4):
                for j in range(3):
                    n = BASE_IN[0] + 1 + 3 * g + j
                    load(n, ring_cols(n), col_chunk(w_in[0], j * D + g * COLS))
            for layer in range(2):
                if layer == 1:
                    load(BASE_IN[1], ring_cols(BASE_IN[1]), col_chunk(w_in[1], 2 * D))
                    for g in range(4):
                        for j in range(2):
                            n = BASE_IN[1] + 1 + 2 * g + j
                            load(n, ring_cols(n), col_chunk(w_in[1], j * D + g * COLS))
                    load_ln(2)
                for c in range(CW):
                    n = BASE_WO[layer] + c
                    load(n, ring_rows(n), w_o[layer].rearrange("(c k p) n -> c p k n", k=PIECE, p=P)[c])
                moe_loads(layer)
                overflow(layer)

            for t in range(TT):
                sp.wait_ge(row_ready, 3 * TT + t + 1)
                sp.dma_start(out[0, t * P:(t + 1) * P, :], xrow[:, t, :]).then_inc(out_done, 16)
            sp.wait_ge(out_done, 16 * TT)

        @block.gpsimd
        def _(pool):
            g = nc.gpsimd
            own = Order(pool, g_order)
            own.mark(g.memset(ident[:, :], 0.0))
            own.mark(g.memset(neg_tri[:, :], -1.0))
            own.mark(g.memset(before[:, :], 1.0))
            own.wait()
            g.affine_select(out=ident[:, :], in_=ident[:, :], compare_op=ALU.not_equal, fill=1.0, base=0,
                            pattern=[[-1, P]], channel_multiplier=1).then_inc(consts, 1)
            g.affine_select(out=neg_tri[:, :], in_=neg_tri[:, :], compare_op=ALU.is_ge, fill=0.0, base=0,
                            pattern=[[-1, P]], channel_multiplier=1).then_inc(consts, 1)
            g.affine_select(out=before[:, :], in_=before[:, :], compare_op=ALU.is_gt, fill=0.0, base=0,
                            pattern=[[1, P]], channel_multiplier=-1).then_inc(consts, 1)
            g.memset(neg_one[:, :], -1.0).then_inc(consts, 1)
            g.memset(ones[:, :], 1.0).then_inc(consts, 1)
            g.memset(minus_half[:, :], -0.5).then_inc(consts, 1)
            g.memset(zero_tab[:, :], 0).then_inc(consts2, 1)
            g.iota(tok_id[:, :], pattern=[[P, TT]], base=0, channel_multiplier=1).then_inc(consts2, 1)
            g.iota(seg_base[:, :, :], pattern=[[0, TT], [S, E]], base=0, channel_multiplier=0,
                   allow_small_or_imprecise_dtypes=True).then_inc(consts2, 1)
            g.iota(near_base[:, :, :], pattern=[[0, TT], [CAP, E]], base=0, channel_multiplier=0,
                   allow_small_or_imprecise_dtypes=True).then_inc(consts2, 1)
            g.iota(rank_e[:, :, :], pattern=[[0, TT], [-1, E]], base=E, channel_multiplier=0,
                   allow_small_or_imprecise_dtypes=True).then_inc(consts2, 1)
            g.iota(rank_g[:, :, :], pattern=[[0, TT], [-1, GROUPS]], base=GROUPS, channel_multiplier=0,
                   allow_small_or_imprecise_dtypes=True).then_inc(consts2, 1)
            pool.wait_ge(consts2, 6)
            for layer in range(2):
                g.dma_start(token_of_slot[layer].rearrange("(p n) a -> p (n a)", p=P), zero_tab[:, :]).then_inc(tab_in, 16)

            for h in range(HEADS):
                for r in range(TT):
                    kb = TT - 1 - r
                    o, _ = blk(kb)
                    pool.wait_ge(soft_v, TT * h + r + 1)
                    g.affine_select(out=soft[:, o:o + P], in_=soft[:, o:o + P], compare_op=ALU.is_gt, fill=0.0, base=0,
                                    pattern=[[1, P]], channel_multiplier=-1).then_inc(soft_g, 1)
                for r in range(TT):
                    o, _ = blk(TT - 1 - r)
                    pool.wait_ge(w_a, TT * h + r + 1)
                    g.affine_select(out=aT[:, o:o + P], in_=aT[:, o:o + P], compare_op=ALU.is_gt, fill=0.0, base=0,
                                    pattern=[[1, P]], channel_multiplier=-1).then_inc(w_g, 1)

            def inverse_root(i):
                for t in range(TT):
                    pool.wait_ge(ln_var, i * TT + t + 1)
                    g.tensor_tensor(rstd[:, t:t + 1], mv[:, t, 1:2], minus_half[:, :], ALU.pow).then_inc(ln_rs, 1)

            pool.wait_ge(consts, 6)
            for layer in range(2):
                if layer == 1:
                    pool.wait_ge(yg_v, 2 * TT)
                    g.memset(hpad[:, :, 0:32], 0.0).then_inc(pad_g, 1)
                inverse_root(2 * layer)
                pool.wait_ge(slots_v, 2 + layer * 2)
                pool.wait_ge(tab_in, 32)
                for k in range(2):
                    for t in range(TT):
                        g.indirect_dma_start(out=token_of_slot[layer], in_=tok_id[:, t:t + 1], in_offset=None,
                                             out_offset=bass.IndirectOffsetOnAxis(ap=slot_i[:, k, t:t + 1], axis=0)
                                             ).then_inc(scat, 16)
                pool.wait_ge(slot_tok_v, 1 + layer)

                def gather(e, r, par, done):
                    at = e * ROUNDS + r
                    g.indirect_dma_start(out=xg[0:CAP, par, :], in_=rows_dram[layer], out_offset=None,
                                         in_offset=bass.IndirectOffsetOnAxis(ap=slot_tok[0:CAP, at:at + 1], axis=0)
                                         ).then_inc(done, 16)

                pool.wait_ge(rows_out, 16 * TT * (layer + 1))
                for e in range(E):
                    if e >= 2:
                        pool.wait_ge(xt_mm, 2 * (e - 1) + 2 * E * layer)
                    gather(e, 0, e % 2, gat[e % 2])

                most_reg = pool.value_load(most[0:1, 0:1], min_val=0, max_val=S)
                with pool.If(most_reg > CAP):
                    for par in range(2):
                        pool.wait_ge(y_st[par], 16 * (E // 2) * (layer + 1))
                    g.memset(xT[:, 0:2, :], 0.0).then_inc(o_clear[layer], 1)
                    pool.wait_ge(o_clear[layer], 1)
                    rows_each = E * S // P
                    g.dma_start(far_dram.rearrange("(n p) d -> p n d", p=P),
                                xT[:, 0:2, :].rearrange("p a b -> p (a b)").unsqueeze(1).to_broadcast([P, rows_each, D])
                                ).then_inc(o_zero[layer], 16)
                    pool.wait_ge(o_zero[layer], 16)
                    for i in range((ROUNDS - 1) * E):
                        pool.wait_ge(o_pe[layer], 4 * i + 4)
                        gather(i % E, i // E + 1, 0, o_x[layer])
                    pool.wait_ge(o_st[layer], 16 * (ROUNDS - 1) * E)
                    for t in range(TT):
                        for k in range(2):
                            j = 2 * t + k
                            if t:
                                pool.wait_ge(o_dve[layer], FAR_DVE + j - 1)
                            g.indirect_dma_start(out=yg[:, k, :], in_=far_dram, out_offset=None,
                                                 in_offset=bass.IndirectOffsetOnAxis(ap=slot_i[:, k, t:t + 1], axis=0)
                                                 ).then_inc(o_far[layer][k], 16)
                    pool.wait_ge(o_dve[layer], FAR_DVE + 2 * TT)

                for par in range(2):
                    pool.wait_ge(y_st[par], 16 * (E // 2) + layer * 8 * E)
                for t in range(TT):
                    for k in range(2):
                        j = 2 * t + k
                        g.indirect_dma_start(out=yg[:, j, :], in_=near_dram[layer], out_offset=None,
                                             in_offset=bass.IndirectOffsetOnAxis(ap=near_i[:, k, t:t + 1], axis=0)
                                             ).then_inc(yg_in[j], 16)
                inverse_root(2 * layer + 1)

        @block.scalar
        def _(act):
            a = nc.scalar
            own = Order(act, a_order)

            def xT_half(i):
                for t in range(TT):
                    act.wait_ge(tp_mm, i * 2 * TT + 2 * t + 1)
                    a.copy(xT[:, 0:4, t * P:(t + 1) * P], ps[:, 4 + (t % 2) * 2, :].rearrange("p (k n) -> p k n", k=4)
                           ).then_inc(xT_a, 1)

            xT_half(0)
            for m in range(MT):
                act.wait_ge(mt_mm, 2 * m + 1)
                a.copy(memT[:, 0:4, m * P:(m + 1) * P], ps[:, 2 * m, :].rearrange("p (k n) -> p k n", k=4)).then_inc(mt_a, 1)
            for j in range(8):
                layer, kind, i = j // 4, (j // 2) % 2, j % 2
                act.wait_ge(*kv_event(j))
                dst = kTm[:, layer, i, :] if kind == 0 else vm[:, layer, i, :]
                a.copy(dst, ps[:, 4 + j % 2, 0:MEM]).then_inc(kv_ev, 1)

            def log_terms(h):
                for r in range(TT):
                    _, n = blk(TT - 1 - r)
                    act.wait_ge(abs_v, TT * h + r + 1)
                    a.activation(lt[:, r % 2, 0:n], lt[:, r % 2, 0:n], ACT.Exp, scale=-1.0).then_inc(e_a, 1)
                    act.wait_ge(e_a, TT * h + r + 1)
                    a.activation(lt[:, r % 2, 0:n], lt[:, r % 2, 0:n], ACT.Ln, bias=1.0).then_inc(l_a, 1)

            def stick_weights(h):
                for r in range(TT):
                    kb = TT - 1 - r
                    o, n = blk(kb)
                    act.wait_ge(c_mm, TT * h + r + 1)
                    if h:
                        act.wait_ge(av_mm, h)
                    a.activation(aT[:, o:o + n], ps[:, 2 + kb, 0:n], ACT.Exp).then_inc(w_a, 1)

            def mem_probs(layer, h):
                act.wait_ge(ms_v, h + 1 + layer * MEM_HEADS)
                for q in range(TT):
                    a.activation(probs[:, q, :], ps[:, mem_bank[layer] + q // 2, (q % 2) * MEM:(q % 2) * MEM + MEM], ACT.Exp,
                                 bias=mstat[:, 0, q:q + 1], scale=MEM_DH ** -0.5, accum_out=mstat[:, 1, q:q + 1]).then_inc(ms_a, 1)

            for h in range(HEADS - 2):
                log_terms(h)
                stick_weights(h)
            for h in range(HEADS - 2, HEADS):
                m = 2 * (h - HEADS + 2)
                mem_probs(0, m)
                log_terms(h)
                mem_probs(0, m + 1)
                stick_weights(h)

            def moe(layer):
                sgb = hact

                def half0(par, e):
                    act.wait_ge(xt_mm, 2 * e + 1 + layer * 2 * E)
                    a.copy(xgT[:, par, 0:4, :], ps[:, 7, :].rearrange("p (k n) -> p k n", k=4)).then_inc(xt_a, 1)

                def silu_gate(par, e):
                    act.wait_ge(chunks_used, first_done(BASE_MOE[layer], e))
                    a.activation(sgb[:, par, :], ps[:, 2 * par, :], ACT.Sigmoid).then_inc(sg_a, 1)

                def out_half(par, e):
                    act.wait_ge(chunks_used, second_done(BASE_MOE[layer], e))
                    if not isinstance(e, int) or e > 1:
                        act.wait_ge(y_st[par], 8 * (e - par) + layer * 8 * E)
                    a.copy(yo[:, par, 0:512], ps[:, 4, :]).then_inc(y_a, 1)
                    act.wait_ge(y_a, e + 1 + layer * E)
                    act.wait_ge(y_v, e + 1 + layer * E)
                    dst = near_dram[layer].rearrange("(e n) d -> e n d", e=E)
                    row = dst[e] if isinstance(e, int) else dst[bass.ds(e, 1)].rearrange("e n d -> (e n) d")
                    act.dma_start(row, yo[0:CAP, par, :]).then_inc(y_st[par], 16)

                def step(par, s):
                    silu_gate(1 - par, s + 1)
                    if not isinstance(s, int) or s < E - 2:
                        half0(par, s + 2)
                    out_half(par, s)

                half0(0, 0)
                silu_gate(0, 0)
                half0(1, 1)
                step(0, 0)
                step(1, 1)
                with act.Fori(0, (E - 4) // 2) as i:
                    step(0, 2 * i + 2)
                    step(1, 2 * i + 3)
                step(0, E - 2)
                out_half(1, E - 1)

                most_reg = act.value_load(most[0:1, 0:1], min_val=0, max_val=S)
                with act.If(most_reg > CAP):
                    for par in range(2):
                        act.wait_ge(y_st[par], 16 * (E // 2) + layer * 8 * E)
                    with act.Fori(0, (ROUNDS - 1) * E) as i:
                        act.wait_ge(o_pe[layer], 4 * i + 4 + 2)
                        a.activation(sgb[:, 0, :], ps[:, 0, :], ACT.Sigmoid).then_inc(o_sg[layer], 1)
                        act.wait_ge(o_dve[layer], 5 * i + 5)
                        dst = far_dram.rearrange("(e r n) d -> r e n d", r=ROUNDS, n=CAP)
                        dst = dst[bass.ds(i // E + 1, 1), bass.ds(i % E, 1)].rearrange("r e n d -> (r e n) d")
                        act.dma_start(dst, yo[0:CAP, 0, :]).then_inc(o_st[layer], 16)
                        act.wait_ge(o_st[layer], 16 * (i + 1))

            for layer in range(2):
                if layer == 1:
                    for j in range(KD + 1):
                        if j < KD and j % 2 == 0:
                            mem_probs(1, j // 2)
                        if j < KD:
                            act.wait_ge(*gate_event(j))
                            if j >= 2:
                                act.wait_ge(gl_v, j - 1)
                            a.activation(gl[:, j % 2, :], ps[:, 2 * (j % 2) + 1, :], ACT.Sigmoid).then_inc(gl_a, 1)
                        if j:
                            ct = j - 1
                            act.wait_ge(cv_mm, PE_TAPS * (ct + 1))
                            a.activation(mixT[:, ct, :], ps[:, 7, :], ACT.Identity, bias=convc[:, ct, TAPS:TAPS + 1]).then_inc(cv_a, 1)
                        if j < KD:
                            if j == 0:
                                act.wait_ge(cc_v, 1)
                            if j >= 2:
                                act.wait_ge(cv_mm, PE_TAPS * (j - 1))
                            for tap in range(PE_TAPS):
                                a.activation(dg[:, PE_TAPS * (j % 2) + tap, :], ident[:, :], ACT.Copy, scale=convc[:, j, tap:tap + 1]
                                             ).then_inc(dg_a, 1)
                    for ct in range(KD):
                        act.wait_ge(yc_v, ct + 1)
                        if ct >= 2:
                            act.wait_ge(var_mm, ct - 1)
                        a.activation(gl[:, ct % 2, :], mixT[:, ct, :], ACT.Square).then_inc(sq_a, 1)
                    act.wait_ge(var_v, 1)
                    a.activation(t0, rs_b, ACT.Ln).then_inc(lnv_a, 1)
                    act.wait_ge(lnv_a, 1)
                    a.activation(t0, t0, ACT.Exp, scale=-0.5).then_inc(lnv_a, 1)
                    for ct in range(KD):
                        act.wait_ge(u_v, ct + 1)
                        if ct >= 2:
                            act.wait_ge(mix_v, ct - 1)
                        a.activation(gl[:, ct % 2, :], mixT[:, ct, :], ACT.Sigmoid).then_inc(su_a, 1)
                xT_half(2 * layer + 1)
                act.wait_ge(rt_mm, 1 + layer)
                a.activation(sc[:, :, :], ps[:, 0, 0:TT * E].rearrange("p (t e) -> p t e", e=E), ACT.Sigmoid).then_inc(sig_a, 1)
                act.wait_ge(scat, 16 * 2 * TT + layer * 16 * 2 * TT)
                tab = token_of_slot[layer].rearrange("(e n) a -> e (n a)", n=CAP)
                act.dma_start(tab_i[:, :], tab).then_inc(tab_ld, 16)
                moe(layer)
                if layer == 0:
                    xT_half(2)

        @block.vector
        def _(dve):
            v_ = nc.vector
            own = Order(dve, v_order)

            def xT_half(i, t):
                dve.wait_ge(tp_mm, i * 2 * TT + 2 * t + 2)
                v_.tensor_copy(xT[:, 4:8, t * P:(t + 1) * P], ps[:, 5 + (t % 2) * 2, :].rearrange("p (k n) -> p k n", k=4)
                               ).then_inc(xT_v, 1)

            for t in range(TT):
                xT_half(0, t)
            for m in range(MT):
                dve.wait_ge(mt_mm, 2 * m + 2)
                v_.tensor_copy(memT[:, 4:8, m * P:(m + 1) * P], ps[:, 1 + 2 * m, :].rearrange("p (k n) -> p k n", k=4)).then_inc(mt_v, 1)

            def mq_evac(j):
                dve.wait_ge(*mq_event(0, j))
                v_.tensor_copy(mqT[:, j, :], ps[:, j % 2, :]).then_inc(pj_ev, 1)

            dve.wait_ge(chunks_used, N_KV)
            mq_evac(0)
            mq_evac(1)

            def qkv_evac(g, i):
                j = 2 + 8 * g + i
                buf = g % 2
                dve.wait_ge(*proj_event(g, i))
                if g >= 2:
                    dve.wait_ge(av_mm, 2 * (g - 1))
                if i < 2:
                    ins = v_.tensor_scalar(qT[:, 2 * buf + i, :], ps[:, j % 2, :], float(P) ** -0.5, None, ALU.mult)
                elif i < 4:
                    ins = v_.tensor_copy(kT[:, 2 * buf + i - 2, :], ps[:, j % 2, :])
                else:
                    ins = v_.tensor_copy(v[:, TT * buf + i - 4, :], ps[:, j % 2, 0:COLS])
                ins.then_inc(pj_ev, 1)

            def head_soft(h, m=None):
                for r in range(TT):
                    kb = TT - 1 - r
                    o, n = blk(kb)
                    dve.wait_ge(z_mm, TT * h + r + 1)
                    if r >= 2:
                        dve.wait_ge(soft_v, TT * h + r - 1)
                    elif h:
                        dve.wait_ge(soft_v, TT * h)
                    v_.tensor_single_scalar(lt[:, r % 2, 0:n].bitcast(I32), ps[:, 2 + kb, 0:n].bitcast(I32), 0x7FFFFFFF,
                                            ALU.bitwise_and).then_inc(abs_v, 1)
                    if m is not None and r == 1:
                        mem_turned(0, m)
                    if r >= 1:
                        soft_out(h, r - 1)
                    if m is not None and r == TT - 1:
                        mem_out(0, m)
                soft_out(h, TT - 1)

            def soft_out(h, r):
                kb = TT - 1 - r
                o, n = blk(kb)
                dve.wait_ge(l_a, TT * h + r + 1)
                if h:
                    dve.wait_ge(c_mm, TT * h)
                v_.scalar_tensor_tensor(out=soft[:, o:o + n], in0=ps[:, 2 + kb, 0:n], scalar=0.0, in1=lt[:, r % 2, 0:n],
                                        op0=ALU.max, op1=ALU.add).then_inc(soft_v, 1)

            def head_out(h):
                dve.wait_ge(av_mm, h + 1)
                v_.tensor_copy(mixT[:, h, :], ps[:, 6 + h % 2, :]).then_inc(av_ev, 1)

            def mem_max(layer, h):
                dve.wait_ge(ms_mm, h + 1 + layer * MEM_HEADS)
                b = mem_bank[layer]
                own.mark(v_.tensor_reduce(mstat[:, 0, :], ps[:, b:b + 2, :].rearrange("p b (q m) -> p (b q) m", q=2), AX_X, ALU.max))
                own.wait()
                v_.tensor_scalar(mstat[:, 0, :], mstat[:, 0, :], -(MEM_DH ** -0.5), None, ALU.mult).then_inc(ms_v, 1)

            def mem_norm(layer, h):
                dve.wait_ge(ms_a, TT * (h + 1) + layer * MEM_HEADS * TT)
                own.mark(v_.reciprocal(mstat[:, 1, :], mstat[:, 1, :]))
                own.wait()
                v_.tensor_tensor(probs[:, :, :], probs[:, :, :], mstat[:, 1, :].unsqueeze(2).to_broadcast([P, TT, MEM]), ALU.mult
                                 ).then_inc(mp_v, 1)

            def mem_turned(layer, h):
                dve.wait_ge(mt2_mm, h + 1 + layer * MEM_HEADS)
                b = mem_bank[layer]
                v_.tensor_copy(pT[:, :, :], ps[:, b:b + 2, :]).then_inc(mt2_v, 1)

            def mem_out(layer, h):
                dve.wait_ge(mo_mm, h + 1 + layer * MEM_HEADS)
                o = MEM_DH * (h % 2)
                v_.tensor_copy(mixT[o:o + MEM_DH, KD + h // 2, :], ps[o:o + MEM_DH, mem_bank[layer], :]).then_inc(mo_v, 1)

            for i in range(8):
                qkv_evac(0, i)
            for g in range(3):
                for step in range(4):
                    h = 2 * g + step // 2
                    if step % 2 == 0:
                        head_soft(h)
                    qkv_evac(g + 1, 2 * step)
                    qkv_evac(g + 1, 2 * step + 1)
                    if step % 2:
                        head_out(h)
            for h in range(HEADS - 2, HEADS):
                m = 2 * (h - HEADS + 2)
                if m == 0:
                    mem_max(0, m)
                    mem_norm(0, m)
                head_soft(h, m)
                mem_max(0, m + 1)
                mem_norm(0, m + 1)
                mem_turned(0, m + 1)
                mem_out(0, m + 1)
                if m == 0:
                    mem_max(0, m + 2)
                    mem_norm(0, m + 2)
                head_out(h)

            def norm_head(i, t):
                own.wait()
                for n in range(2):
                    own.mark(v_.bn_stats(stats[:, t, n, :], xrow[:, t, n * 512:(n + 1) * 512]))
                own.wait()
                own.mark(v_.bn_aggr(mv[:, t, :], stats[:, t, :, :].rearrange("p a b -> p (a b)")))
                own.wait()
                v_.tensor_scalar(mv[:, t, 1:2], mv[:, t, 1:2], LN_EPS, None, ALU.add).then_inc(ln_var, 1)

            def norm_mid(i, t):
                if t == 0:
                    dve.wait_ge(ln_in, 32 * (i + 1))
                own.mark(v_.scalar_tensor_tensor(out=xrow[:, t, :], in0=xrow[:, t, :], scalar=mv[:, t, 0:1], in1=lnp[:, 0, :],
                                                 op0=ALU.subtract, op1=ALU.mult))
                dve.wait_ge(ln_rs, i * TT + t + 1)
                own.wait()
                v_.scalar_tensor_tensor(out=xrow[:, t, :], in0=xrow[:, t, :], scalar=rstd[:, t:t + 1], in1=lnp[:, 1, :],
                                        op0=ALU.mult, op1=ALU.add).then_inc(row_ready, 1)

            def residual(layer):
                for t in range(TT):
                    for n in range(2):
                        j = 2 * t + n
                        dve.wait_ge(*out_event(layer, j))
                        cols = slice(n * 512, n * 512 + 512)
                        v_.scalar_tensor_tensor(out=xrow[:, t, cols], in0=xrow[:, t, cols], scalar=ALPHA, in1=ps[:, j % 4, :],
                                                op0=ALU.mult, op1=ALU.add).then_inc(op_v, 1)
                    dve.wait_ge(op_v, 2 * t + 2 + layer * 2 * TT)
                    norm_head(2 * layer, t)
                    norm_mid(2 * layer, t)
                    if t >= 2:
                        xT_half(2 * layer + 1, t - 2)
                xT_half(2 * layer + 1, TT - 2)
                xT_half(2 * layer + 1, TT - 1)

            def route(layer):
                def step(ins):
                    own.mark(ins)
                    own.wait()

                def best(vals, rank, onehot, n):
                    step(v_.tensor_reduce(top[:, :], vals, AX_X, ALU.max))
                    wide = top[:, :].unsqueeze(2).to_broadcast([P, TT, n])
                    key = ekey[:, :, 0:n]
                    step(v_.tensor_tensor(key, vals, wide, ALU.is_equal))
                    step(v_.tensor_tensor(key, key, rank, ALU.mult))
                    step(v_.tensor_reduce(top[:, :], key, AX_X, ALU.max))
                    step(v_.tensor_tensor(onehot, key, wide, ALU.is_equal))

                dve.wait_ge(small_in, 16 * (1 + TT))
                dve.wait_ge(consts2, 6)
                dve.wait_ge(sig_a, 1 + layer)
                step(v_.tensor_tensor(scb[:, :, :], sc[:, :, :], rb[:, :, :], ALU.add))
                by4 = scb[:, :, :].rearrange("p t (g e) -> p (t g) e", e=PER_GROUP)
                own.mark(v_.tensor_tensor(pair[:, :, 0:3], by4[:, :, 0:3], by4[:, :, 1:4], ALU.add))
                own.mark(v_.tensor_tensor(pair[:, :, 3:5], by4[:, :, 0:2], by4[:, :, 2:4], ALU.add))
                step(v_.tensor_tensor(pair[:, :, 5:6], by4[:, :, 0:1], by4[:, :, 3:4], ALU.add))
                step(v_.tensor_reduce(gs[:, :, :].rearrange("p t g -> p (t g)"), pair[:, :, :], AX_X, ALU.max))
                best(gs[:, :, :], rank_g[:, :, :], ge[:, :, :], GROUPS)
                step(v_.tensor_scalar(ge[:, :, :], ge[:, :, :], 1.0, BIG, ALU.subtract, ALU.mult))
                step(v_.tensor_tensor(by4, by4, ge[:, :, :].rearrange("p t g -> p (t g)").unsqueeze(2)
                                      .to_broadcast([P, TT * GROUPS, PER_GROUP]), ALU.add))
                best(scb[:, :, :], rank_e[:, :, :], oh1[:, :, :], E)
                step(v_.scalar_tensor_tensor(out=scb[:, :, :], in0=oh1[:, :, :], scalar=-4.0 * BIG, in1=scb[:, :, :],
                                             op0=ALU.mult, op1=ALU.add))
                best(scb[:, :, :], rank_e[:, :, :], oh2[:, :, :], E)
                v_.tensor_tensor(both[:, :, :], oh1[:, :, :], oh2[:, :, :], ALU.add).then_inc(pick_v, 1)
                for k, oh in enumerate((oh1, oh2)):
                    step(v_.tensor_tensor(ekey[:, :, :], sc[:, :, :], oh[:, :, :], ALU.mult))
                    step(v_.tensor_reduce(gate[:, k, :], ekey[:, :, :], AX_X, ALU.add))
                step(v_.tensor_tensor(gsum[:, :], gate[:, 0, :], gate[:, 1, :], ALU.add))
                step(v_.reciprocal(gsum[:, :], gsum[:, :]))
                for k in range(2):
                    step(v_.tensor_tensor(gate[:, k, :], gate[:, k, :], gsum[:, :], ALU.mult))
                dve.wait_ge(pos_mm, 1 + layer)
                pos = ps[:, 5, 0:TT * E].rearrange("p (t e) -> p t e", e=E)
                step(v_.tensor_tensor(scb[:, :, :], pos, seg_base[:, :, :], ALU.add))
                for k, oh in enumerate((oh1, oh2)):
                    step(v_.tensor_tensor(ekey[:, :, :], scb[:, :, :], oh[:, :, :], ALU.mult))
                    step(v_.tensor_reduce(slot_f[:, k, :], ekey[:, :, :], AX_X, ALU.add))
                v_.tensor_copy(slot_i[:, :, :], slot_f[:, :, :]).then_inc(slots_v, 1)
                step(v_.tensor_reduce(most_f[:, :], ps[:, 5, TT * E:TT * E + E], AX_X, ALU.max))
                v_.tensor_copy(most[:, :], most_f[:, :]).then_inc(slots_v, 1)
                step(v_.tensor_scalar(over[:, :, :], pos, float(CAP), float(2 * E * S), ALU.is_ge, ALU.mult))
                step(v_.tensor_tensor(over[:, :, :], over[:, :, :], near_base[:, :, :], ALU.add))
                step(v_.tensor_tensor(over[:, :, :], over[:, :, :], pos, ALU.add))
                for k, oh in enumerate((oh1, oh2)):
                    step(v_.tensor_tensor(ekey[:, :, :], over[:, :, :], oh[:, :, :], ALU.mult))
                    step(v_.tensor_reduce(near_f[:, k, :], ekey[:, :, :], AX_X, ALU.add))
                step(v_.tensor_scalar(near_gate[:, :, :], near_f[:, :, :], float(E * S), None, ALU.is_lt))
                step(v_.tensor_tensor(near_f[:, :, :], near_f[:, :, :], near_gate[:, :, :], ALU.mult))
                step(v_.tensor_copy(near_i[:, :, :], near_f[:, :, :]))
                step(v_.tensor_tensor(near_gate[:, :, :], near_gate[:, :, :], gate[:, :, :], ALU.mult))
                dve.wait_ge(tab_ld, 16 + layer * 16)
                v_.tensor_copy(tab_f[:, :], tab_i[:, :]).then_inc(tabf_v, 1)
                dve.wait_ge(tab_mm, 1 + layer)
                v_.tensor_copy(slot_tok[0:CAP, :], ps[0:CAP, 5, 128:128 + E * ROUNDS]).then_inc(slot_tok_v, 1)

            def moe(layer):
                def half1(par, e):
                    dve.wait_ge(xt_mm, 2 * e + 2 + layer * 2 * E)
                    v_.tensor_copy(xgT[:, par, 4:8, :], ps[:, 6, :].rearrange("p (k n) -> p k n", k=4)).then_inc(xt_v, 1)

                def activate(par, e):
                    dve.wait_ge(sg_a, e + 1 + layer * E)
                    v_.tensor_tensor(hact[:, par, :], hact[:, par, :], ps[:, 2 * par, :], ALU.mult).then_inc(sg_v, 1)
                    dve.wait_ge(sg_v, e + 1 + layer * E)
                    v_.tensor_tensor(hact[:, par, :], hact[:, par, :], ps[:, 2 * par + 1, :], ALU.mult).then_inc(h_v, 1)

                def hT_evac(par, e):
                    dve.wait_ge(ht_mm, e + 1 + layer * E)
                    v_.tensor_copy(hT[:, par, :, :], ps[:, 6, :].rearrange("p (k n) -> p k n", k=4)).then_inc(ht_v, 1)

                def out_half(par, e):
                    dve.wait_ge(chunks_used, second_done(BASE_MOE[layer], e))
                    if not isinstance(e, int) or e > 1:
                        dve.wait_ge(y_st[par], 8 * (e - par) + layer * 8 * E)
                    v_.tensor_copy(yo[:, par, 512:1024], ps[:, 5, :]).then_inc(y_v, 1)

                def step(par, s):
                    hT_evac(par, s)
                    activate(1 - par, s + 1)
                    if not isinstance(s, int) or s < E - 2:
                        half1(par, s + 2)
                    out_half(par, s)

                half1(0, 0)
                activate(0, 0)
                half1(1, 1)
                step(0, 0)
                dve.wait_ge(rows_out, 16 * TT * (layer + 1))
                for t in range(TT):
                    own.mark(v_.tensor_scalar(xrow[:, t, :], xrow[:, t, :], ALPHA, None, ALU.mult))
                own.wait()
                step(1, 1)
                with dve.Fori(0, (E - 4) // 2) as i:
                    step(0, 2 * i + 2)
                    step(1, 2 * i + 3)
                step(0, E - 2)
                hT_evac(1, E - 1)
                out_half(1, E - 1)

                most_reg = dve.value_load(most[0:1, 0:1], min_val=0, max_val=S)
                with dve.If(most_reg > CAP):
                    for par in range(2):
                        dve.wait_ge(y_st[par], 16 * (E // 2) + layer * 8 * E)
                    with dve.Fori(0, (ROUNDS - 1) * E) as i:
                        dve.wait_ge(o_pe[layer], 4 * i + 4 + 1)
                        v_.tensor_copy(xgT[:, 0, :, :], ps[:, 6:8, :].rearrange("p b (k n) -> p (b k) n", k=4)).then_inc(o_dve[layer], 1)
                        dve.wait_ge(o_sg[layer], i + 1)
                        v_.tensor_tensor(hact[:, 0, :], hact[:, 0, :], ps[:, 0, :], ALU.mult).then_inc(o_dve[layer], 1)
                        dve.wait_ge(o_dve[layer], 5 * i + 2)
                        v_.tensor_tensor(hact[:, 0, :], hact[:, 0, :], ps[:, 1, :], ALU.mult).then_inc(o_dve[layer], 1)
                        dve.wait_ge(o_pe[layer], 4 * i + 4 + 3)
                        v_.tensor_copy(hT[:, 0, :, :], ps[:, 2, :].rearrange("p (k n) -> p k n", k=4)).then_inc(o_dve[layer], 1)
                        dve.wait_ge(o_pe[layer], 4 * i + 4 + 4)
                        v_.tensor_copy(yo[:, 0, :], ps[:, 4:6, :].rearrange("p b n -> p (b n)")).then_inc(o_dve[layer], 1)
                    v_.tensor_tensor(far_gate[:, :, :], gate[:, :, :], near_gate[:, :, :], ALU.subtract).then_inc(o_dve[layer], 1)
                    dve.wait_ge(o_dve[layer], FAR_DVE)
                    for t in range(TT):
                        for k in range(2):
                            dve.wait_ge(o_far[layer][k], 16 * (t + 1))
                            v_.scalar_tensor_tensor(out=xrow[:, t, :], in0=yg[:, k, :], scalar=far_gate[:, k, t:t + 1], in1=xrow[:, t, :],
                                                    op0=ALU.mult, op1=ALU.add).then_inc(o_dve[layer], 1)
                            dve.wait_ge(o_dve[layer], FAR_DVE + 2 * t + k + 1)

            def combine(layer):
                i = 2 * layer + 1
                for t in range(TT):
                    for k in range(2):
                        dve.wait_ge(yg_in[2 * t + k], 16 * (layer + 1))
                        v_.scalar_tensor_tensor(out=xrow[:, t, :], in0=yg[:, 2 * t + k, :], scalar=near_gate[:, k, t:t + 1],
                                                in1=xrow[:, t, :], op0=ALU.mult, op1=ALU.add).then_inc(yg_v, 1)
                        dve.wait_ge(yg_v, 2 * t + k + 1 + layer * 2 * TT)
                    norm_head(i, t)
                    norm_mid(i, t)

            def conv_taps(ct, first, last):
                for tap in range(first, last):
                    if tap > PE_TAPS + 1:
                        dve.wait_ge(v_order, own.n - 1)
                    elif tap == PE_TAPS:
                        dve.wait_ge(cv_a, ct + 1)
                    src, weight = hpad[:, ct, 2 + tap:2 + tap + S], convc[:, ct, tap:tap + 1]
                    total = t0 if (tap - PE_TAPS) % 2 else mixT[:, ct, :]
                    if tap == PE_TAPS + 1:
                        own.mark(v_.tensor_scalar(total, src, weight, None, ALU.mult))
                    else:
                        own.mark(v_.scalar_tensor_tensor(out=total, in0=src, scalar=weight, in1=total, op0=ALU.mult, op1=ALU.add))
                if last == TAPS:
                    own.wait()
                    v_.tensor_tensor(mixT[:, ct, :], mixT[:, ct, :], t0, ALU.add).then_inc(cv_v, 1)
                    dve.wait_ge(cv_v, ct + 1)

            def conv_layer():
                mid = (PE_TAPS + TAPS) // 2
                dve.wait_ge(pad_g, 1)
                for j in range(2):
                    dve.wait_ge(*mq_event(1, j))
                    v_.tensor_copy(mqT[:, j, :], ps[:, 4 + j, :]).then_inc(mq_v, 1)
                dve.wait_ge(cc_mm, 2)
                v_.tensor_copy(convc[:, :, :], ps[:, 6:8, :].rearrange("p b (k n) -> p (b k) n", n=P)[:, :, 0:TAPS + 3]).then_inc(cc_v, 1)
                dve.wait_ge(cc_v, 1)
                mem_max(1, 0)
                mem_norm(1, 0)
                for j in range(KD + 1):
                    if j < KD:
                        dve.wait_ge(*gate_event(j))
                        dve.wait_ge(gl_a, j + 1)
                        v_.tensor_tensor(hpad[:, j, 32:32 + S], gl[:, j % 2, :], ps[:, 2 * (j % 2), :], ALU.mult).then_inc(gl_v, 1)
                        dve.wait_ge(gl_v, j + 1)
                    if j % 2:
                        mem_out(1, j // 2)
                    elif j < KD:
                        mem_turned(1, j // 2)
                    if j:
                        conv_taps(j - 1, PE_TAPS, mid)
                    if j % 2 and j < KD - 1:
                        mem_max(1, j // 2 + 1)
                    if j:
                        conv_taps(j - 1, mid, TAPS)
                    if j % 2 and j < KD - 1:
                        mem_norm(1, j // 2 + 1)
                dve.wait_ge(mu_mm, 1)
                v_.tensor_scalar(mean_b, ps[:, 6, :], 1.0 / D, None, ALU.mult).then_inc(mu_v, 1)
                dve.wait_ge(mu_v, 1)
                for ct in range(KD):
                    v_.tensor_tensor(mixT[:, ct, :], mixT[:, ct, :], mean_b, ALU.subtract).then_inc(yc_v, 1)
                dve.wait_ge(var_mm, KD)
                v_.tensor_scalar(rs_b, ps[:, 3, :], 1.0 / D, LN_EPS, ALU.mult, ALU.add).then_inc(var_v, 1)
                dve.wait_ge(lnv_a, 2)
                own.mark(v_.tensor_tensor(t1, t0, t0, ALU.mult))
                own.wait()
                own.mark(v_.tensor_tensor(t1, t1, rs_b, ALU.mult))
                own.wait()
                own.mark(v_.tensor_scalar(t1, t1, -0.5, 1.5, ALU.mult, ALU.add))
                own.wait()
                v_.tensor_tensor(rs_b, t1, t0, ALU.mult).then_inc(rsb_v, 1)
                dve.wait_ge(rsb_v, 1)
                for ct in range(KD):
                    own.mark(v_.tensor_tensor(mixT[:, ct, :], mixT[:, ct, :], rs_b, ALU.mult))
                    own.wait()
                    v_.tensor_scalar(mixT[:, ct, :], mixT[:, ct, :], convc[:, ct, TAPS + 1:TAPS + 2], convc[:, ct, TAPS + 2:TAPS + 3],
                                     ALU.mult, ALU.add).then_inc(u_v, 1)
                    if ct:
                        finish(ct - 1)
                finish(KD - 1)

            def finish(ct):
                dve.wait_ge(su_a, ct + 1)
                v_.tensor_tensor(mixT[:, ct, :], mixT[:, ct, :], gl[:, ct % 2, :], ALU.mult).then_inc(mix_v, 1)

            for layer in range(2):
                if layer == 1:
                    conv_layer()
                residual(layer)
                route(layer)
                moe(layer)
                combine(layer)
                if layer == 0:
                    for t in range(TT):
                        xT_half(2, t)

        @block.tensor
        def _(pe):
            t_ = nc.tensor

            def x_transpose(i, t):
                if i:
                    pe.wait_ge(row_ready, (i - 1) * TT + t + 1)
                if t >= 2:
                    pe.wait_ge(xT_a, i * TT + t - 1)
                    pe.wait_ge(xT_v, i * TT + t - 1)
                for b in range(2):
                    for k in range(4):
                        ins = t_.transpose(ps[:, 4 + (t % 2) * 2 + b, k * P:(k + 1) * P],
                                           xrow[:, t, (4 * b + k) * P:(4 * b + k + 1) * P], ident[:, :])
                    ins.then_inc(tp_mm, 1)

            pe.wait_ge(consts, 6)
            pe.wait_ge(x_in, 16 * TT)
            for t in range(TT):
                x_transpose(0, t)
            pe.wait_ge(mem_in, 16)
            for m in range(MT):
                for b in range(2):
                    for k in range(4):
                        ins = t_.transpose(ps[:, 2 * m + b, k * P:(k + 1) * P],
                                           memrow[:, m, (4 * b + k) * P:(4 * b + k + 1) * P], ident[:, :])
                    ins.then_inc(mt_mm, 1)
            pe.wait_ge(mt_a, MT)
            pe.wait_ge(mt_v, MT)

            for j in range(8):
                layer, kind, i = j // 4, (j // 2) % 2, j % 2
                n = 2 * layer + kind
                pe.wait_ge(landed[slot_of(n)], loaded(n))
                if j >= 2:
                    pe.wait_ge(kv_ev, j - 1)
                elif j == 0:
                    pe.wait_ge(xT_a, TT)
                    pe.wait_ge(xT_v, TT)
                w = ring_cols(n)
                for k in range(KD):
                    if kind == 0:
                        ins = t_.matmul(ps[:, 4 + j % 2, 0:MEM], w[:, k, i * P:(i + 1) * P], memT[:, k, :],
                                        start=(k == 0), stop=(k == KD - 1))
                    else:
                        ins = t_.matmul(ps[:, 4 + j % 2, 0:MEM], memT[:, k, i * P:(i + 1) * P], w[:, k, :],
                                        start=(k == 0), stop=(k == KD - 1))
                ins.then_inc(kv_event(j)[0], 1)

            def feature_tile(bank, n, i):
                pe.wait_ge(landed[slot_of(n)], loaded(n))
                w = ring_cols(n)
                for k in range(KD):
                    ins = t_.matmul(ps[:, bank, :], w[:, k, i * P:(i + 1) * P], xT[:, k, :], start=(k == 0), stop=(k == KD - 1))
                return ins

            for j in range(2):
                feature_tile(j, BASE_IN[0], j).then_inc(mq_event(0, j)[0], 1)

            def project(g, i):
                j = 2 + 8 * g + i
                n = BASE_IN[0] + 1 + 3 * g + min(i // 2, 2)
                pe.wait_ge(pj_ev, j - 1)
                if i < 4:
                    ins = feature_tile(j % 2, n, i % 2)
                else:
                    pe.wait_ge(landed[slot_of(n)], loaded(n))
                    w, t = ring_cols(n), i - 4
                    for k in range(KD):
                        ins = t_.matmul(ps[:, j % 2, 0:COLS], xT[:, k, t * P:(t + 1) * P], w[:, k, :],
                                        start=(k == 0), stop=(k == KD - 1))
                ins.then_inc(proj_event(g, i)[0], 1)

            def scores(h):
                buf = 2 * ((h // 2) % 2) + h % 2
                pe.wait_ge(pj_ev, 2 + 8 * (h // 2 + 1))
                if h == 0:
                    pe.wait_ge(kv_ev, 8)
                for r in range(TT):
                    kb = TT - 1 - r
                    n = blk(kb)[1]
                    if h:
                        pe.wait_ge(w_a, TT * (h - 1) + r + 1)
                    t_.matmul(ps[:, 2 + kb, 0:n], kT[:, buf, kb * P:(kb + 1) * P], qT[:, buf, kb * P:S],
                              start=True, stop=True).then_inc(z_mm, 1)

            def later_sums(h):
                for r in range(TT):
                    kb = TT - 1 - r
                    pe.wait_ge(soft_g, TT * h + r + 1)
                    pe.wait_ge(soft_v, TT * h + r + 1)
                    for other in range(TT - 1, kb - 1, -1):
                        o, n = blk(other)
                        at = (other - kb) * P
                        ins = t_.matmul(ps[:, 2 + kb, at:at + n], (neg_tri if other == kb else neg_one)[:, :], soft[:, o:o + n],
                                        start=False, stop=True, skip_group_check=True)
                    ins.then_inc(c_mm, 1)

            def weigh(h):
                g, i = h // 2, h % 2
                if h >= 2:
                    pe.wait_ge(av_ev, h - 1)
                pe.wait_ge(w_g, TT * (h + 1))
                pe.wait_ge(w_a, TT * (h + 1))
                for kb in range(TT):
                    o, n = blk(kb)
                    ins = t_.matmul(ps[:, 6 + i, kb * P:S], v[:, TT * (g % 2) + kb, i * P:(i + 1) * P], aT[:, o:o + n],
                                    start=(kb == 0), stop=(kb == TT - 1))
                ins.then_inc(av_mm, 1)

            for i in range(8):
                project(0, i)
            def mem_scores(layer, h):
                hp, o = h // 2, MEM_DH * (h % 2)
                if h:
                    pe.wait_ge(mo_v, h + layer * MEM_HEADS)
                for q in range(TT):
                    ins = t_.matmul(ps[:, mem_bank[layer] + q // 2, (q % 2) * MEM:(q % 2) * MEM + MEM],
                                    mqT[o:o + MEM_DH, hp, q * P:(q + 1) * P], kTm[o:o + MEM_DH, layer, hp, :],
                                    start=True, stop=True)
                ins.then_inc(ms_mm, 1)

            def mem_turn(layer, h):
                pe.wait_ge(mp_v, h + 1 + layer * MEM_HEADS)
                for q in range(TT):
                    for m in range(MT):
                        ins = t_.transpose(ps[:, mem_bank[layer] + m, q * P:(q + 1) * P], probs[:, q, m * P:(m + 1) * P], ident[:, :])
                ins.then_inc(mt2_mm, 1)

            def mem_weigh(layer, h):
                o = MEM_DH * (h % 2)
                pe.wait_ge(mt2_v, h + 1 + layer * MEM_HEADS)
                for m in range(MT):
                    ins = t_.matmul(ps[o:o + MEM_DH, mem_bank[layer], :], vm[:, layer, m, h * MEM_DH:(h + 1) * MEM_DH],
                                    pT[:, m, :], start=(m == 0), stop=(m == MT - 1))
                ins.then_inc(mo_mm, 1)

            for g in range(3):
                for step in range(4):
                    h = 2 * g + step // 2
                    if step % 2 == 0:
                        scores(h)
                    project(g + 1, 2 * step)
                    project(g + 1, 2 * step + 1)
                    if step % 2 == 0:
                        later_sums(h)
                    else:
                        weigh(h)
            pe.wait_ge(pj_ev, 2 + 8 * 4)
            mem_scores(0, 0)
            for h in range(HEADS - 2, HEADS):
                m = 2 * (h - HEADS + 2)
                scores(h)
                mem_turn(0, m)
                mem_weigh(0, m)
                mem_scores(0, m + 1)
                later_sums(h)
                mem_turn(0, m + 1)
                mem_weigh(0, m + 1)
                if m == 0:
                    mem_scores(0, m + 2)
                weigh(h)

            def out_project(layer):
                for t in range(TT):
                    for n in range(2):
                        j = 2 * t + n
                        if j >= 4:
                            pe.wait_ge(op_v, j - 3 + layer * 2 * TT)
                        for k in range(MIX_TILES):
                            c = BASE_WO[layer] + k // PIECE
                            if j == 0 and k % PIECE == 0:
                                pe.wait_ge(landed[slot_of(c)], loaded(c))
                            ins = t_.matmul(ps[:, j % 4, :], mixT[:, k, t * P:(t + 1) * P], ring_rows(c)[:, k % PIECE, n * 512:(n + 1) * 512],
                                            start=(k == 0), stop=(k == MIX_TILES - 1))
                        if j < 2 * TT - 1:
                            ins.then_inc(op_mm, 1)
                        else:
                            ins.then_inc(chunks_used, CW)
                    if t:
                        x_transpose(2 * layer + 1, t - 1)
                x_transpose(2 * layer + 1, TT - 1)

            def route(layer):
                pe.wait_ge(op_v, (layer + 1) * 2 * TT)
                for t in range(TT):
                    pe.wait_ge(xT_a, (2 * layer + 1) * TT + t + 1)
                    pe.wait_ge(xT_v, (2 * layer + 1) * TT + t + 1)
                    for k in range(KD):
                        ins = t_.matmul(ps[:, 0, t * E:(t + 1) * E], xT[:, k, t * P:(t + 1) * P], rw[:, k, :],
                                        start=(k == 0), stop=(k == KD - 1))
                ins.then_inc(rt_mm, 1)
                pe.wait_ge(pick_v, 1 + layer)
                for t in range(TT):
                    for u in range(t + 1):
                        t_.matmul(ps[:, 5, t * E:(t + 1) * E], (before if u == t else ones)[:, :], both[:, u, :],
                                  start=(u == 0), stop=(u == t))
                for u in range(TT):
                    ins = t_.matmul(ps[:, 5, TT * E:TT * E + E], ones[:, :], both[:, u, :], start=(u == 0), stop=(u == TT - 1))
                ins.then_inc(pos_mm, 1)
                pe.wait_ge(tabf_v, 1 + layer)
                rows = E * ROUNDS
                t_.transpose(ps[0:CAP, 5, 128:128 + rows], tab_f[:, :], ident[0:rows, 0:rows]).then_inc(tab_mm, 1)

            def moe(layer):
                base = BASE_MOE[layer]

                def rows_transpose(par, e, half):
                    if half == 0:
                        pe.wait_ge(gat[par], 8 * (e - par) + 16 + layer * 8 * E)
                        if not isinstance(e, int) or e > 0:
                            pe.wait_ge(xt_a, e + layer * E)
                    else:
                        if not isinstance(e, int) or e > 0:
                            pe.wait_ge(xt_v, e + layer * E)
                        if not isinstance(e, int) or e > 1:
                            pe.wait_ge(ht_v, e - 1 + layer * E)
                    bank = 7 - half
                    for k in range(4):
                        ins = t_.transpose(ps[:, bank, k * P:k * P + CAP], xg[0:CAP, par, (4 * half + k) * P:(4 * half + k + 1) * P],
                                           ident[0:CAP, 0:CAP])
                    ins.then_inc(xt_mm, 1)

                def first_product(par, e, n0, s, c):
                    n = n0 + c
                    pe.wait_ge(landed[slot_of(n)], 16 * s + loaded(n))
                    if c == 0:
                        if isinstance(e, int) and e == 0:
                            pe.wait_ge(sig_a, 1 + layer)
                        pe.wait_ge(xt_a, e + 1 + layer * E)
                        pe.wait_ge(xt_v, e + 1 + layer * E)
                        if not isinstance(e, int) or e > 1:
                            pe.wait_ge(h_v, e - 1 + layer * E)
                    w = ring_rows(n)
                    for k in range(PIECE):
                        for half in range(2):
                            kk = PIECE * c + k
                            ins = t_.matmul(ps[0:CAP, 2 * par + half, :], xgT[:, par, kk, :], w[:, k, half * 512:(half + 1) * 512],
                                            start=(kk == 0), stop=(kk == KD - 1))
                    ins.then_inc(chunks_used, 1)

                def h_transpose(par, e):
                    pe.wait_ge(h_v, e + 1 + layer * E)
                    if not isinstance(e, int) or e < E - 1:
                        pe.wait_ge(xt_v, e + 2 + layer * E)
                    for k in range(FK):
                        ins = t_.transpose(ps[:, 6, k * P:k * P + CAP], hact[0:CAP, par, k * P:(k + 1) * P], ident[0:CAP, 0:CAP])
                    ins.then_inc(ht_mm, 1)

                def second_product(par, e, n0, s):
                    pe.wait_ge(ht_v, e + 1 + layer * E)
                    if not isinstance(e, int) or e > 0:
                        pe.wait_ge(y_a, e + layer * E)
                        pe.wait_ge(y_v, e + layer * E)
                    for c in range(CB):
                        n = n0 + c
                        pe.wait_ge(landed[slot_of(n)], 16 * s + loaded(n))
                        w = ring_rows(n)
                        for k in range(PIECE):
                            for half in range(2):
                                kk = PIECE * c + k
                                ins = t_.matmul(ps[0:CAP, 4 + half, :], hT[:, par, kk, :], w[:, k, half * 512:(half + 1) * 512],
                                                start=(kk == 0), stop=(kk == FK - 1))
                        ins.then_inc(chunks_used, 1)

                def step(par, s):
                    n0 = base + CA
                    for c in range(CA):
                        first_product(1 - par, s + 1, n0, s, c)
                        if c == 0:
                            h_transpose(par, s)
                    if not isinstance(s, int) or s < E - 2:
                        rows_transpose(par, s + 2, 0)
                        rows_transpose(par, s + 2, 1)
                    second_product(par, s, n0 + CA, s)

                pe.wait_ge(slot_tok_v, 1 + layer)
                rows_transpose(0, 0, 0)
                rows_transpose(0, 0, 1)
                for c in range(CA):
                    first_product(0, 0, base, 0, c)
                rows_transpose(1, 1, 0)
                rows_transpose(1, 1, 1)
                step(0, 0)
                step(1, 1)
                with pe.Fori(0, (E - 4) // 2) as i:
                    step(0, 2 * i + 2)
                    step(1, 2 * i + 3)
                step(0, E - 2)
                h_transpose(1, E - 1)
                second_product(1, E - 1, base + E * STEP - CB, 0)

                most_reg = pe.value_load(most[0:1, 0:1], min_val=0, max_val=S)
                with pe.If(most_reg > CAP):
                    pe.wait_ge(y_a, E + layer * E)
                    pe.wait_ge(y_v, E + layer * E)
                    pe.nop().then_inc(o_pe[layer], 4)
                    with pe.Fori(0, (ROUNDS - 1) * E) as i:
                        pe.wait_ge(o_x[layer], 16 * i + 16)
                        for k in range(KD):
                            ins = t_.transpose(ps[:, 6 + k // 4, (k % 4) * P:(k % 4) * P + CAP], xg[0:CAP, 0, k * P:(k + 1) * P],
                                               ident[0:CAP, 0:CAP])
                        ins.then_inc(o_pe[layer], 1)
                        pe.wait_ge(o_dve[layer], 5 * i + 1)
                        pe.wait_ge(o_w[layer], 16 * STEP * i + 16 * STEP)
                        for k in range(KD):
                            for half in range(2):
                                ins = t_.matmul(ps[0:CAP, half, :], xgT[:, 0, k, :], ring_rows(k // PIECE)[:, k % PIECE, half * 512:half * 512 + 512],
                                                start=(k == 0), stop=(k == KD - 1))
                        ins.then_inc(o_pe[layer], 1)
                        pe.wait_ge(o_dve[layer], 5 * i + 3)
                        for k in range(FK):
                            ins = t_.transpose(ps[:, 2, k * P:k * P + CAP], hact[0:CAP, 0, k * P:(k + 1) * P], ident[0:CAP, 0:CAP])
                        ins.then_inc(o_pe[layer], 1)
                        pe.wait_ge(o_dve[layer], 5 * i + 4)
                        for k in range(FK):
                            for half in range(2):
                                ins = t_.matmul(ps[0:CAP, 4 + half, :], hT[:, 0, k, :],
                                                ring_rows(CA + k // PIECE)[:, k % PIECE, half * 512:half * 512 + 512],
                                                start=(k == 0), stop=(k == FK - 1))
                        ins.then_inc(o_pe[layer], 1)

            def convolution():
                for j in range(2):
                    feature_tile(4 + j, BASE_IN[1], j).then_inc(mq_event(1, j)[0], 1)
                pe.wait_ge(conv_in, 16 * 4)
                rows = TAPS + 3
                for k in range(KD):
                    ins = t_.transpose(ps[:, 6 + k // 4, (k % 4) * P:(k % 4) * P + rows], conv_rows[:, k * P:(k + 1) * P],
                                       ident[0:rows, 0:rows])
                    if k % 4 == 3:
                        ins.then_inc(cc_mm, 1)
                pe.wait_ge(mq_v, 2)
                for j in range(KD + 1):
                    h = j // 2
                    if j < KD:
                        if j % 2:
                            mem_turn(1, h)
                        if j >= 2:
                            pe.wait_ge(gl_v, j - 1)
                        a_chunk = BASE_IN[1] + 1 + 2 * h
                        ins = feature_tile(2 * (j % 2), a_chunk, j % 2)
                        if j % 2:
                            ins.then_inc(chunks_used, 1)
                        else:
                            mem_scores(1, h)
                        feature_tile(2 * (j % 2) + 1, a_chunk + 1, j % 2).then_inc(gate_event(j)[0], 1)
                        if j % 2:
                            mem_weigh(1, h)
                    if j:
                        ct = j - 1
                        pe.wait_ge(gl_v, j)
                        if ct:
                            pe.wait_ge(cv_a, ct)
                        else:
                            pe.wait_ge(cc_v, 1)
                        for tap in range(PE_TAPS):
                            pe.wait_ge(dg_a, ct * PE_TAPS + tap + 1)
                            t_.matmul(ps[:, 7, :], dg[:, PE_TAPS * (ct % 2) + tap, :], hpad[:, ct, 2 + tap:2 + tap + S],
                                      start=(tap == 0), stop=(tap == PE_TAPS - 1)).then_inc(cv_mm, 1)
                for ct in range(KD):
                    pe.wait_ge(cv_v, ct + 1)
                    ins = t_.matmul(ps[:, 6, :], ones[:, :], mixT[:, ct, :], start=(ct == 0), stop=(ct == KD - 1))
                ins.then_inc(mu_mm, 1)
                for ct in range(KD):
                    pe.wait_ge(sq_a, ct + 1)
                    t_.matmul(ps[:, 3, :], ones[:, :], gl[:, ct % 2, :], start=(ct == 0), stop=(ct == KD - 1)).then_inc(var_mm, 1)
                pe.wait_ge(var_v, 1)

            for layer in range(2):
                if layer == 1:
                    pe.wait_ge(xT_a, 2 * TT + TT)
                    pe.wait_ge(xT_v, 2 * TT + TT)
                    convolution()
                if layer == 1:
                    pe.wait_ge(mix_v, KD)
                else:
                    pe.wait_ge(av_ev, HEADS)
                pe.wait_ge(mo_v, MEM_HEADS * (layer + 1))
                out_project(layer)
                route(layer)
                moe(layer)
                if layer == 0:
                    for t in range(TT):
                        x_transpose(2, t)


INPUTS = ["x", "mem", "router_w", "router_bias",
          "l0_w_in", "l0_mem_wkv", "l0_w_o", "l0_ln_g", "l0_ln_b", "l0_moe_w_in", "l0_moe_w_out",
          "l1_w_in", "l1_conv_w", "l1_conv_b", "l1_conv_norm_g", "l1_conv_norm_b", "l1_mem_wkv", "l1_w_o",
          "l1_ln_g", "l1_ln_b", "l1_moe_w_in", "l1_moe_w_out"]


def kernel(**inputs):
    import numpy as _np
    import concourse.bacc as _bacc
    from concourse import mybir as _mybir
    from concourse.bass_utils import run_bass_kernel_spmd as _run

    nc = _bacc.Bacc("TRN2", target_bir_lowering=False, num_devices=1)
    arrays, args = {}, []
    for name in INPUTS:
        a = _np.ascontiguousarray(inputs[name])
        arrays[f"in_{name}"] = a
        args.append(nc.dram_tensor(f"in_{name}", a.shape, _mybir.dt.from_np(a.dtype), kind="ExternalInput").ap())
    out = nc.dram_tensor("out_x", (1, S, D), _mybir.dt.from_np(_np.dtype("float32")), kind="ExternalOutput").ap()
    build(nc, *args, out)
    r = _run(nc, [arrays], core_ids=[0])
    return r.results[0]["out_x"]
```

```python
from contextlib import ExitStack

import concourse.bass as bass
from concourse import mybir

ALU = mybir.AluOpType
ACT = mybir.ActivationFunctionType
AX_X = mybir.AxisListType.X
F32 = mybir.dt.float32
I32 = mybir.dt.int32
BF16 = mybir.dt.bfloat16
F32R = mybir.dt.float32r

P = 128
S, D = 512, 1024
TT, KD = S // P, D // P
MEM = 256
MT = MEM // P
HEADS = 8
MEM_HEADS, MEM_DH = 4, 64
MEM_TILES = MEM_HEADS * MEM_DH // P
MIX_TILES = D // P + MEM_TILES
MIX_ORDER = [(i + D // P) % MIX_TILES for i in range(MIX_TILES)]
TAPS = 31
PE_TAPS = [7] * (D // P - 2) + [8, 12]
TAPS_BEFORE = [sum(PE_TAPS[:i]) for i in range(D // P + 1)]
DIAGS = 12
E, GROUPS, PER_GROUP, FF = 16, 4, 4, 512
FK = FF // P
ALPHA = (2.0 * 2) ** 0.25
LN_EPS = 1e-5
BIG = 1e30

SLOTS = 6
COLS = 256
PIECE = 2
CA = KD // PIECE
CB = FK // PIECE
CW = MIX_TILES // PIECE
N_KV = 4
N_IN = (1 + 3 * 4, 9)
STEP = CA + CB
BASE_IN = (N_KV, N_KV + N_IN[0] + CW + E * STEP)
BASE_WO = (BASE_IN[0] + N_IN[0], BASE_IN[1] + N_IN[1])
BASE_MOE = (BASE_WO[0] + CW, BASE_WO[1] + CW)

CAP = 128
ROUNDS = S // CAP


PER_TABLE = 4
TABLES = E // PER_TABLE
FAR_DVE = 5 * (ROUNDS - 1) * E + 1


def slot_of(n):
    return n % SLOTS


def loaded(n):
    return 16 * (n // SLOTS + 1)


def first_done(base, e):
    return base + CA if isinstance(e, int) and e == 0 else base + 2 * CA - STEP + STEP * e


def second_done(base, e):
    return base + E * STEP if isinstance(e, int) and e == E - 1 else STEP * e + (base + CA + STEP)


class Order:

    def __init__(self, engine, semaphore):
        self.engine, self.semaphore, self.n = engine, semaphore, 0

    def mark(self, instruction):
        instruction.then_inc(self.semaphore, 1)
        self.n = self.n + 1

    def wait(self):
        self.engine.wait_ge(self.semaphore, self.n)


def build(nc, x, mem, router_w, router_bias,
          l0_w_in, l0_mem_wkv, l0_w_o, l0_ln_g, l0_ln_b, l0_moe_w_in, l0_moe_w_out,
          l1_w_in, l1_conv_w, l1_conv_b, l1_conv_norm_g, l1_conv_norm_b, l1_mem_wkv, l1_w_o,
          l1_ln_g, l1_ln_b, l1_moe_w_in, l1_moe_w_out, out):
    w_in, mem_wkv, w_o = (l0_w_in, l1_w_in), (l0_mem_wkv, l1_mem_wkv), (l0_w_o, l1_w_o)
    ln_g, ln_b = (l0_ln_g, l1_ln_g), (l0_ln_b, l1_ln_b)
    moe_in, moe_out = (l0_moe_w_in, l1_moe_w_in), (l0_moe_w_out, l1_moe_w_out)

    rows_dram = [nc.dram_tensor(f"rows{i}", [S, D], F32, kind="Internal").ap() for i in range(2)]
    near_dram = [nc.dram_tensor(f"near{i}", [E * CAP, D], F32, kind="Internal").ap() for i in range(2)]
    far_dram = nc.dram_tensor("far", [E * S, D], F32, kind="Internal").ap()

    with ExitStack() as ctx:
        def sb(name, shape, dt=F32):
            return ctx.enter_context(nc.sbuf_tensor(name, shape, dt))

        def sem(name):
            return ctx.enter_context(nc.semaphore(name))

        def two(name):
            return [sem(f"{name}{i}") for i in range(2)]

        ps = ctx.enter_context(nc.psum_tensor("ps", [P, 8, 512], F32))

        xrow = sb("xrow", [P, TT, D])
        xh, xl = sb("xh", [P, KD, S], F32R), sb("xl", [P, KD, S], F32R)
        wh, wl = sb("wh", [P, KD, 2, P], F32R), sb("wl", [P, KD, 2, P], F32R)
        mixT = sb("mixT", [P, MIX_TILES, S])
        ring = sb("ring", [P, SLOTS, 2048])
        mqT = sb("mqT", [P, 2, S])
        kTm = sb("kTm", [P, 2, 2, MEM])
        vm = sb("vm", [P, 2, MT, MEM])
        lnp = sb("lnp", [P, 2, D])
        ident = sb("ident", [P, P])
        neg_tri = sb("neg_tri", [P, P])
        neg_one = sb("neg_one", [P, P])
        ones = sb("ones", [P, P])
        before = sb("before", [P, P], BF16)
        ones_b = sb("ones_b", [P, P], BF16)
        rw = sb("rw", [P, KD, E])
        rb = sb("rb", [P, TT, E])
        tok_id = sb("tok_id", [P, TT, 2], BF16)
        one_up = sb("one_up", [P, CAP])
        seg_base = sb("seg_base", [P, TT, E])
        rank_e = sb("rank_e", [P, TT, E])
        rank_g = sb("rank_g", [P, TT, GROUPS])
        minus_half = sb("minus_half", [P, 1])
        stats = sb("stats", [P, TT, 2, 6])
        mv = sb("mv", [P, TT, 2])
        rstd = sb("rstd", [P, TT])
        lt = sb("lt", [P, 2, S])
        probs, pT = sb("probs", [P, TT, MEM]), sb("pT", [P, MT, S])
        mstat = sb("mstat", [P, 2, TT])

        sc = sb("sc", [P, TT, E])
        scb = sb("scb", [P, TT, E])
        pair = sb("pair", [P, TT * GROUPS, 6])
        gs = sb("gs", [P, TT, GROUPS])
        ge = sb("ge", [P, TT, GROUPS])
        top = sb("top", [P, TT])
        ekey = sb("ekey", [P, TT, E])
        oh1 = sb("oh1", [P, TT, E])
        oh2 = sb("oh2", [P, TT, E])
        both = sb("both", [P, TT + 1, E], BF16)
        gate = sb("gate", [P, 2, TT])
        gsum = sb("gsum", [P, TT])
        slot_f = sb("slot_f", [P, 2, TT])
        slot_i = sb("slot_i", [P, 2, TT], I32)
        near_base = sb("near_base", [P, TT, E])
        near_f, near_gate, far_gate = sb("near_f", [P, 2, TT]), sb("near_gate", [P, 2, TT]), sb("far_gate", [P, 2, TT])
        near_i = sb("near_i", [P, 2, TT], I32)
        most_f = sb("most_f", [P, 1])
        most = sb("most", [P, 1], I32)
        place = sb("place", [P, TT, E])
        tok_f = sb("tok_f", [P, E])
        slot_tok = sb("slot_tok", [P, ROUNDS, E], I32)

        arena = sb("arena", [P, 8960])

        def part(start, *shape):
            size = 1
            for n in shape:
                size *= n
            flat = arena[:, start:start + size]
            if len(shape) == 1:
                return flat
            names = "abc"[:len(shape)]
            return flat.rearrange(f"p ({' '.join(names)}) -> p {' '.join(names)}", **dict(zip(names, shape)))

        memrow, memT = part(0, MT, D), part(2048, KD, MEM)
        qT, kT, v = part(0, 4, S), part(2048, 4, S), part(4096, 8, COLS)
        soft, aT = part(6144, 1280), part(7424, 1280)
        HP = S + 32
        hpad = part(0, KD, HP)
        cv = KD * HP
        gl = part(cv, 2, S)
        mean_b, rs_b, t0, t1 = (part(cv + 2 * S + i * S, S) for i in range(4))
        dg = part(cv + 6 * S, DIAGS, P)
        xT = part(0, KD, S)
        xg, xgT = part(0, 2, D), part(2048, 2, KD, CAP)
        hact, hT, yo = part(4096, 2, FF), part(5120, 2, FK, CAP), part(6144, 2, D)
        yg = part(0, 2 * TT, D)
        xh_f, xl_f = (t[:, :, :].rearrange("p k n -> p (k n)") for t in (xh, xl))
        wh_f, wl_f = (t[:, :, :, :].rearrange("p k i n -> p (k i n)") for t in (wh, wl))
        out_h = [wh_f[:, 0:D], wh_f[:, D:2 * D], xh_f[:, 2 * D:3 * D], xh_f[:, 3 * D:4 * D]]
        out_l = [wl_f[:, 0:D], wl_f[:, D:2 * D], xl_f[:, 2 * D:3 * D], xl_f[:, 3 * D:4 * D]]
        hTh, hTl = (f[:, 0:2 * FK * CAP].rearrange("p (i k n) -> p i k n", i=2, k=FK) for f in (xh_f, xl_f))
        match = arena[:, 6144:8192].bitcast(BF16).rearrange("p (i t e s) -> p i t e s", i=2, t=TT, e=PER_TABLE)
        mem_bank = (0, 4)
        conv_rows = lt[0:TAPS + 3, :, :].rearrange("p a n -> p (a n)")
        convc = sb("convc", [P, KD, TAPS + 3])

        landed = [sem(f"landed{i}") for i in range(SLOTS)]
        chunks_used = sem("chunks_used")
        x_in, mem_in, small_in, conv_in = sem("x_in"), sem("mem_in"), sem("small_in"), sem("conv_in")
        ln_in = sem("ln_in")
        consts, consts2 = sem("consts"), sem("consts2")
        v_order, a_order, g_order = sem("v_order"), sem("a_order"), sem("g_order")
        tp_mm, xT_a, xT_v = sem("tp_mm"), sem("xT_a"), sem("xT_v")
        xh_a, xl_v, wh_a, wl_v, wl_g = (sem(n) for n in ("xh_a", "xl_v", "wh_a", "wl_v", "wl_g"))
        a_mm = sem("a_mm")
        out_h_a, out_l_v, hTh_v = sem("out_h_a"), sem("out_l_v"), sem("hTh_v")
        mt_mm, mt_a, mt_v = sem("mt_mm"), sem("mt_a"), sem("mt_v")
        kv_mm, kv_ev = sem("kv_mm"), sem("kv_ev")
        pj_mm, pj_ev = sem("pj_mm"), sem("pj_ev")
        z_mm, abs_v, e_a, l_a, soft_v, soft_g, c_mm, w_a, w_g, av_mm, av_ev = (
            sem(n) for n in ("z_mm", "abs_v", "e_a", "l_a", "soft_v", "soft_g", "c_mm", "w_a", "w_g", "av_mm", "av_ev"))
        ms_mm, ms_v, ms_a, mp_v, mt2_mm, mt2_v, mo_mm, mo_v = (
            sem(n) for n in ("ms_mm", "ms_v", "ms_a", "mp_v", "mt2_mm", "mt2_v", "mo_mm", "mo_v"))
        op_mm, op_v = sem("op_mm"), sem("op_v")
        ln_var, ln_rs, row_ready = sem("ln_var"), sem("ln_rs"), sem("row_ready")
        rows_out = sem("rows_out")
        rt_mm, sig_a, pick_v, pos_mm, slots_v, match_v, tab_mm, tok_v, slot_tok_v = (
            sem(n) for n in ("rt_mm", "sig_a", "pick_v", "pos_mm", "slots_v", "match_v", "tab_mm", "tok_v", "slot_tok_v"))
        gat = two("gat")
        xt_mm, xt_a, xt_v, sg_a, sg_v, h_v, ht_mm, ht_v, y_a, y_v = (
            sem(n) for n in ("xt_mm", "xt_a", "xt_v", "sg_a", "sg_v", "h_v", "ht_mm", "ht_v", "y_a", "y_v"))
        y_st = two("y_st")
        o_clear, o_zero = two("o_clear"), two("o_zero")
        o_match, o_tab = two("o_match"), two("o_tab")
        o_far = [two("o_far_l0_"), two("o_far_l1_")]
        o_w, o_x, o_pe, o_dve, o_sg, o_st = (two(n) for n in ("o_w", "o_x", "o_pe", "o_dve", "o_sg", "o_st"))
        yg_in = [sem(f"yg_in{k}") for k in range(2 * TT)]
        yg_v = sem("yg_v")
        pad_g = sem("pad_g")
        cc_mm, cc_v = sem("cc_mm"), sem("cc_v")
        mq_mm = two("mq_mm")
        gl_mm, gl_a, gl_v = sem("gl_mm"), sem("gl_a"), sem("gl_v")
        mq_v = sem("mq_v")
        dg_a, cv_mm, cv_v = sem("dg_a"), sem("cv_mm"), sem("cv_v")
        mu_mm, mu_v, yc_v, sq_a, var_mm, var_v, lnv_a, rsb_v, z_g, su_a, mix_v = (
            sem(n) for n in ("mu_mm", "mu_v", "yc_v", "sq_a", "var_mm", "var_v", "lnv_a", "rsb_v", "z_g", "su_a", "mix_v"))
        out_done = sem("out_done")

        block = ctx.enter_context(nc.Block())

        def kv_event(j):
            return (chunks_used, j // 2 + 1) if j % 2 else (kv_mm, j // 2 + 1)

        def mq_event(layer, j):
            return (chunks_used, BASE_IN[layer] + 1) if j else (mq_mm[layer], 1)

        def proj_event(g, i):
            first = BASE_IN[0] + 1 + 3 * g
            if i in (1, 3, 7):
                return chunks_used, first + {1: 1, 3: 2, 7: 3}[i]
            return pj_mm, 5 * g + {0: 1, 2: 2, 4: 3, 5: 4, 6: 5}[i]

        def gate_event(j):
            return (chunks_used, BASE_IN[1] + 1 + 2 * (j // 2 + 1)) if j % 2 else (gl_mm, j // 2 + 1)

        def out_event(layer, j):
            return (chunks_used, BASE_MOE[layer]) if j == 2 * TT - 1 else (op_mm, j + 1 + layer * (2 * TT - 1))

        units = [(BASE_IN[0], i, mq_event(0, i)) for i in range(2)]
        for g in range(4):
            for r in range(6):
                units.append((BASE_IN[0] + 1 + 3 * g + r // 2, r % 2, proj_event(g, r if r < 4 else 7)))
        UNITS_1 = len(units)
        units += [(BASE_IN[1], i, mq_event(1, i)) for i in range(2)]
        for j in range(KD):
            a_chunk = BASE_IN[1] + 1 + 2 * (j // 2)
            units.append((a_chunk, j % 2, (chunks_used, a_chunk + 1) if j % 2 else (a_mm, j // 2 + 1)))
            units.append((a_chunk + 1, j % 2, gate_event(j)))

        def unit_raw(u):
            chunk, half, _ = units[u]
            return ring_cols(chunk)[:, :, half * P:(half + 1) * P]

        def col_chunk(w, c0):
            return w[:, c0:c0 + COLS].rearrange("(k p) n -> p k n", p=P)

        def ring_cols(n):
            return ring[:, slot_of(n), :].rearrange("p (k n) -> p k n", n=COLS)

        def ring_rows(n):
            return ring[:, slot_of(n), :].rearrange("p (k n) -> p k n", n=D)

        def expert_rows(w, e, c):
            view = w.rearrange("e (c k p) n -> c e p k n", k=PIECE, p=P)[c]
            if isinstance(e, int):
                return view[e]
            return view[bass.ds(e, 1)].rearrange("e p k n -> p (e k) n")

        def blk(kb):
            start = sum((TT - j) * P for j in range(kb))
            return start, (TT - kb) * P

        @block.sync
        def _(sp):
            xt = x[0].rearrange("(t p) d -> p t d", p=P)
            for t in range(TT):
                sp.dma_start(xrow[:, t, :], xt[:, t, :]).then_inc(x_in, 16)
            sp.dma_start(memrow, mem[0].rearrange("(t p) d -> p t d", p=P)).then_inc(mem_in, 16)

            def load(n, dst, src):
                if n >= SLOTS:
                    sp.wait_ge(chunks_used, n - SLOTS + 1)
                sp.dma_start(dst, src).then_inc(landed[slot_of(n)], 16)

            for layer in range(2):
                for j in range(2):
                    load(2 * layer + j, ring_cols(2 * layer + j), col_chunk(mem_wkv[layer], j * COLS))
            sp.dma_start(rw[:, :, :], router_w.rearrange("(k p) e -> p k e", p=P)).then_inc(small_in, 16)
            for t in range(TT):
                sp.dma_start(rb[:, t, :], router_bias.partition_broadcast(P)).then_inc(small_in, 16)

            def load_ln(i):
                layer, which = i // 2, i % 2
                if i:
                    sp.wait_ge(row_ready, (i - 1) * TT + TT)
                sp.dma_start(lnp[:, 0, :], ln_g[layer][which].partition_broadcast(P)).then_inc(ln_in, 16)
                sp.dma_start(lnp[:, 1, :], ln_b[layer][which].partition_broadcast(P)).then_inc(ln_in, 16)

            load_ln(0)

            def moe_loads(layer):
                base = BASE_MOE[layer]
                for c in range(CA):
                    load(base + c, ring_rows(base + c), expert_rows(moe_in[layer], 0, c))
                for t in range(TT):
                    sp.wait_ge(row_ready, (2 * layer) * TT + t + 1)
                    sp.dma_start(rows_dram[layer][t * P:(t + 1) * P, :], xrow[:, t, :]).then_inc(rows_out, 16)
                load_ln(2 * layer + 1)

                def step(s, e_next, e_last):
                    for c in range(STEP):
                        n = base + CA + c
                        src = expert_rows(moe_in[layer], e_next, c) if c < CA else expert_rows(moe_out[layer], e_last, c - CA)
                        sp.wait_ge(chunks_used, s * STEP + (n - SLOTS + 1))
                        sp.dma_start(ring_rows(n), src).then_inc(landed[slot_of(n)], 16)

                with sp.Fori(0, E - 1) as s:
                    step(s, s + 1, s)
                n0 = base + E * STEP - CB
                for c in range(CB):
                    load(n0 + c, ring_rows(n0 + c), expert_rows(moe_out[layer], E - 1, c))

            def overflow(layer):
                sp.wait_ge(slots_v, 2 + layer * 2)
                most_reg = sp.value_load(most[0:1, 0:1], min_val=0, max_val=S)
                with sp.If(most_reg > CAP):
                    sp.wait_ge(chunks_used, BASE_MOE[layer] + E * STEP)
                    with sp.Fori(0, (ROUNDS - 1) * E) as i:
                        e = i % E
                        for c in range(STEP):
                            src = expert_rows(moe_in[layer], e, c) if c < CA else expert_rows(moe_out[layer], e, c - CA)
                            sp.wait_ge(o_pe[layer], 4 * i + 4)
                            sp.dma_start(ring_rows(c), src).then_inc(o_w[layer], 16)
                    sp.wait_ge(o_pe[layer], 4 * (ROUNDS - 1) * E + 4)

            load(BASE_IN[0], ring_cols(BASE_IN[0]), col_chunk(w_in[0], 3 * D))
            for g in range(4):
                for j in range(3):
                    n = BASE_IN[0] + 1 + 3 * g + j
                    load(n, ring_cols(n), col_chunk(w_in[0], j * D + g * COLS))
            for layer in range(2):
                if layer == 1:
                    sp.wait_ge(soft_v, TT * HEADS)
                    sp.dma_start(conv_rows[0:TAPS, :], l1_conv_w).then_inc(conv_in, 16)
                    for i, row in enumerate((l1_conv_b, l1_conv_norm_g, l1_conv_norm_b)):
                        sp.dma_start(conv_rows[TAPS + i:TAPS + i + 1, :], row.rearrange("(a n) -> a n", a=1)).then_inc(conv_in, 16)
                    load(BASE_IN[1], ring_cols(BASE_IN[1]), col_chunk(w_in[1], 2 * D))
                    for g in range(4):
                        for j in range(2):
                            n = BASE_IN[1] + 1 + 2 * g + j
                            load(n, ring_cols(n), col_chunk(w_in[1], j * D + g * COLS))
                    load_ln(2)
                for c in range(CW):
                    n = BASE_WO[layer] + c
                    load(n, ring_rows(n), w_o[layer].rearrange("(c k p) n -> c p k n", k=PIECE, p=P)[MIX_ORDER[c * PIECE] // PIECE])
                moe_loads(layer)
                overflow(layer)

            for t in range(TT):
                sp.wait_ge(row_ready, 3 * TT + t + 1)
                sp.dma_start(out[0, t * P:(t + 1) * P, :], xrow[:, t, :]).then_inc(out_done, 16)
            sp.wait_ge(out_done, 16 * TT)

        @block.gpsimd
        def _(pool):
            g = nc.gpsimd
            own = Order(pool, g_order)
            own.mark(g.memset(ident[:, :], 0.0))
            own.mark(g.memset(neg_tri[:, :], -1.0))
            own.mark(g.memset(before[:, :], 1.0))
            own.wait()
            g.affine_select(out=ident[:, :], in_=ident[:, :], compare_op=ALU.not_equal, fill=1.0, base=0,
                            pattern=[[-1, P]], channel_multiplier=1).then_inc(consts, 1)
            g.affine_select(out=neg_tri[:, :], in_=neg_tri[:, :], compare_op=ALU.is_ge, fill=0.0, base=0,
                            pattern=[[-1, P]], channel_multiplier=1).then_inc(consts, 1)
            g.affine_select(out=before[:, :], in_=before[:, :], compare_op=ALU.is_gt, fill=0.0, base=0,
                            pattern=[[1, P]], channel_multiplier=-1).then_inc(consts, 1)
            g.memset(neg_one[:, :], -1.0).then_inc(consts, 1)
            g.memset(ones[:, :], 1.0).then_inc(consts, 1)
            g.memset(minus_half[:, :], -0.5).then_inc(consts, 1)
            g.memset(ones_b[:, :], 1.0).then_inc(consts2, 1)
            g.memset(both[:, TT, :], 0.0).then_inc(consts2, 1)
            g.iota(tok_id[:, :, 0], pattern=[[0, TT]], base=0, channel_multiplier=1,
                   allow_small_or_imprecise_dtypes=True).then_inc(consts2, 1)
            g.iota(tok_id[:, :, 1], pattern=[[P, TT]], base=0, channel_multiplier=0,
                   allow_small_or_imprecise_dtypes=True).then_inc(consts2, 1)
            g.iota(one_up[:, :], pattern=[[1, CAP]], base=1, channel_multiplier=0,
                   allow_small_or_imprecise_dtypes=True).then_inc(consts2, 1)
            g.iota(seg_base[:, :, :], pattern=[[0, TT], [S, E]], base=0, channel_multiplier=0,
                   allow_small_or_imprecise_dtypes=True).then_inc(consts2, 1)
            g.iota(near_base[:, :, :], pattern=[[0, TT], [CAP, E]], base=0, channel_multiplier=0,
                   allow_small_or_imprecise_dtypes=True).then_inc(consts2, 1)
            g.iota(rank_e[:, :, :], pattern=[[0, TT], [-1, E]], base=E, channel_multiplier=0,
                   allow_small_or_imprecise_dtypes=True).then_inc(consts2, 1)
            g.iota(rank_g[:, :, :], pattern=[[0, TT], [-1, GROUPS]], base=GROUPS, channel_multiplier=0,
                   allow_small_or_imprecise_dtypes=True).then_inc(consts2, 1)

            for h in range(HEADS):
                for r in range(TT):
                    kb = TT - 1 - r
                    o, _ = blk(kb)
                    pool.wait_ge(soft_v, TT * h + r + 1)
                    g.affine_select(out=soft[:, o:o + P], in_=soft[:, o:o + P], compare_op=ALU.is_gt, fill=0.0, base=0,
                                    pattern=[[1, P]], channel_multiplier=-1).then_inc(soft_g, 1)
                for r in range(TT):
                    o, _ = blk(TT - 1 - r)
                    pool.wait_ge(w_a, TT * h + r + 1)
                    g.affine_select(out=aT[:, o:o + P], in_=aT[:, o:o + P], compare_op=ALU.is_gt, fill=0.0, base=0,
                                    pattern=[[1, P]], channel_multiplier=-1).then_inc(w_g, 1)

            def inverse_root(i):
                for t in range(TT):
                    pool.wait_ge(ln_var, i * TT + t + 1)
                    g.tensor_tensor(rstd[:, t:t + 1], mv[:, t, 1:2], minus_half[:, :], ALU.pow).then_inc(ln_rs, 1)

            pool.wait_ge(consts, 6)
            for layer in range(2):
                if layer == 1:
                    pool.wait_ge(yg_v, 2 * TT)
                    g.memset(hpad[:, :, 0:32], 0.0).then_inc(pad_g, 1)
                    for u in range(UNITS_1, len(units)):
                        pool.wait_ge(wh_a, u + 1)
                        g.tensor_tensor(wl[:, :, u % 2, :], unit_raw(u), wh[:, :, u % 2, :].bitcast(F32), ALU.subtract
                                        ).then_inc(wl_g, 1)
                    pool.wait_ge(rsb_v, 1)
                    for ct in range(KD):
                        g.tensor_tensor(mixT[:, ct, :], mixT[:, ct, :], rs_b, ALU.mult).then_inc(z_g, 1)
                inverse_root(2 * layer)
                def gather(e, r, par, done):
                    g.indirect_dma_start(out=xg[0:CAP, par, :], in_=rows_dram[layer], out_offset=None,
                                         in_offset=bass.IndirectOffsetOnAxis(ap=slot_tok[0:CAP, r, e:e + 1], axis=0)
                                         ).then_inc(done, 16)

                pool.wait_ge(rows_out, 16 * TT * (layer + 1))
                for e in range(E):
                    if e % PER_TABLE == 0:
                        pool.wait_ge(slot_tok_v, e // PER_TABLE + 1 + TABLES * layer)
                    if e >= 2:
                        pool.wait_ge(xt_mm, 2 * (e - 1) + 2 * E * layer)
                    gather(e, 0, e % 2, gat[e % 2])

                pool.wait_ge(slots_v, 2 + layer * 2)
                most_reg = pool.value_load(most[0:1, 0:1], min_val=0, max_val=S)
                with pool.If(most_reg > CAP):
                    for par in range(2):
                        pool.wait_ge(y_st[par], 16 * (E // 2) * (layer + 1))
                    g.memset(xg[:, 0, :], 0.0).then_inc(o_clear[layer], 1)
                    pool.wait_ge(o_clear[layer], 1)
                    rows_each = E * S // P
                    g.dma_start(far_dram.rearrange("(n p) d -> p n d", p=P),
                                xg[:, 0:1, :].to_broadcast([P, rows_each, D])
                                ).then_inc(o_zero[layer], 16)
                    pool.wait_ge(o_zero[layer], 16)
                    pool.wait_ge(o_match[layer], (3 + TABLES) * (ROUNDS - 1))
                    for i in range((ROUNDS - 1) * E):
                        pool.wait_ge(o_pe[layer], 4 * i + 4)
                        gather(i % E, i // E + 1, 0, o_x[layer])
                    pool.wait_ge(o_st[layer], 16 * (ROUNDS - 1) * E)
                    for t in range(TT):
                        for k in range(2):
                            j = 2 * t + k
                            if t:
                                pool.wait_ge(o_dve[layer], FAR_DVE + j - 1)
                            g.indirect_dma_start(out=yg[:, k, :], in_=far_dram, out_offset=None,
                                                 in_offset=bass.IndirectOffsetOnAxis(ap=slot_i[:, k, t:t + 1], axis=0)
                                                 ).then_inc(o_far[layer][k], 16)
                    pool.wait_ge(o_dve[layer], FAR_DVE + 2 * TT)

                for par in range(2):
                    pool.wait_ge(y_st[par], 16 * (E // 2) + layer * 8 * E)
                for t in range(TT):
                    for k in range(2):
                        j = 2 * t + k
                        g.indirect_dma_start(out=yg[:, j, :], in_=near_dram[layer], out_offset=None,
                                             in_offset=bass.IndirectOffsetOnAxis(ap=near_i[:, k, t:t + 1], axis=0)
                                             ).then_inc(yg_in[j], 16)
                inverse_root(2 * layer + 1)

        @block.scalar
        def _(act):
            a = nc.scalar
            own = Order(act, a_order)

            def xT_half(layer):
                for t in range(TT):
                    act.wait_ge(tp_mm, (2 * layer + 1) * 2 * TT + 2 * t + 1)
                    a.copy(xT[:, 0:4, t * P:(t + 1) * P], ps[:, 4 + (t % 2) * 2, :].rearrange("p (k n) -> p k n", k=4)
                           ).then_inc(xT_a, 1)

            def x_high(layer):
                for t in range(TT):
                    for b in range(2):
                        act.wait_ge(tp_mm, 2 * layer * 2 * TT + 2 * t + b + 1)
                        a.copy(xh[:, 4 * b:4 * b + 4, t * P:(t + 1) * P],
                               ps[:, 4 + (t % 2) * 2 + b, :].rearrange("p (k n) -> p k n", k=4)).then_inc(xh_a, 1)

            def w_high(u):
                chunk = units[u][0]
                act.wait_ge(landed[slot_of(chunk)], loaded(chunk))
                if u >= 2:
                    act.wait_ge(*units[u - 2][2])
                a.copy(wh[:, :, u % 2, :], unit_raw(u)).then_inc(wh_a, 1)

            x_high(0)
            for m in range(MT):
                act.wait_ge(mt_mm, 2 * m + 1)
                a.copy(memT[:, 0:4, m * P:(m + 1) * P], ps[:, 2 * m, :].rearrange("p (k n) -> p k n", k=4)).then_inc(mt_a, 1)
            w_high(0)
            w_high(1)
            for j in range(8):
                layer, kind, i = j // 4, (j // 2) % 2, j % 2
                act.wait_ge(*kv_event(j))
                dst = kTm[:, layer, i, :] if kind == 0 else vm[:, layer, i, :]
                a.copy(dst, ps[:, 4 + j % 2, 0:MEM]).then_inc(kv_ev, 1)

            def log_terms(h):
                for r in range(TT):
                    _, n = blk(TT - 1 - r)
                    act.wait_ge(abs_v, TT * h + r + 1)
                    a.activation(lt[:, r % 2, 0:n], lt[:, r % 2, 0:n], ACT.Exp, scale=-1.0).then_inc(e_a, 1)
                    act.wait_ge(e_a, TT * h + r + 1)
                    a.activation(lt[:, r % 2, 0:n], lt[:, r % 2, 0:n], ACT.Ln, bias=1.0).then_inc(l_a, 1)

            def stick_weights(h):
                for r in range(TT):
                    kb = TT - 1 - r
                    o, n = blk(kb)
                    act.wait_ge(c_mm, TT * h + r + 1)
                    if h:
                        act.wait_ge(av_mm, h)
                    a.activation(aT[:, o:o + n], ps[:, 2 + kb, 0:n], ACT.Exp).then_inc(w_a, 1)

            def mem_probs(layer, h):
                act.wait_ge(ms_v, h + 1 + layer * MEM_HEADS)
                for q in range(TT):
                    a.activation(probs[:, q, :], ps[:, mem_bank[layer] + q // 2, (q % 2) * MEM:(q % 2) * MEM + MEM], ACT.Exp,
                                 bias=mstat[:, 0, q:q + 1], scale=MEM_DH ** -0.5, accum_out=mstat[:, 1, q:q + 1]).then_inc(ms_a, 1)

            for u in range(2, 8):
                w_high(u)
            for h in range(HEADS - 2):
                u = 8 + 6 * (h // 2) + 4 * (h % 2)
                w_high(u)
                w_high(u + 1)
                log_terms(h)
                if h % 2 == 0:
                    w_high(u + 2)
                    w_high(u + 3)
                stick_weights(h)
            for h in range(HEADS - 2, HEADS):
                m = 2 * (h - HEADS + 2)
                mem_probs(0, m)
                log_terms(h)
                mem_probs(0, m + 1)
                stick_weights(h)

            def moe(layer):
                sgb = hact

                def half0(par, e):
                    act.wait_ge(xt_mm, 2 * e + 1 + layer * 2 * E)
                    a.copy(xgT[:, par, 0:4, :], ps[:, 7, :].rearrange("p (k n) -> p k n", k=4)).then_inc(xt_a, 1)

                def silu_gate(par, e):
                    act.wait_ge(chunks_used, first_done(BASE_MOE[layer], e))
                    a.activation(sgb[:, par, :], ps[:, 2 * par, :], ACT.Sigmoid).then_inc(sg_a, 1)

                def out_half(par, e):
                    act.wait_ge(chunks_used, second_done(BASE_MOE[layer], e))
                    if not isinstance(e, int) or e > 1:
                        act.wait_ge(y_st[par], 8 * (e - par) + layer * 8 * E)
                    a.copy(yo[:, par, 0:512], ps[:, 4, :]).then_inc(y_a, 1)
                    act.wait_ge(y_a, e + 1 + layer * E)
                    act.wait_ge(y_v, e + 1 + layer * E)
                    dst = near_dram[layer].rearrange("(e n) d -> e n d", e=E)
                    row = dst[e] if isinstance(e, int) else dst[bass.ds(e, 1)].rearrange("e n d -> (e n) d")
                    act.dma_start(row, yo[0:CAP, par, :]).then_inc(y_st[par], 16)

                def out_high(e, k, last=False):
                    n0, s = (BASE_MOE[layer] + E * STEP - CB, 0) if last else (BASE_MOE[layer] + 2 * CA, e)
                    n = n0 + k // PIECE
                    act.wait_ge(landed[slot_of(n)], 16 * s + loaded(n))
                    if not isinstance(e, int) or e > 0:
                        act.wait_ge(chunks_used, second_done(BASE_MOE[layer], e - 1))
                    a.copy(out_h[k], ring_rows(n)[:, k % PIECE, :]).then_inc(out_h_a, 1)

                def step(par, s):
                    out_high(s, 0)
                    out_high(s, 1)
                    silu_gate(1 - par, s + 1)
                    out_high(s, 2)
                    out_high(s, 3)
                    if not isinstance(s, int) or s < E - 2:
                        half0(par, s + 2)
                    out_half(par, s)

                half0(0, 0)
                silu_gate(0, 0)
                half0(1, 1)
                step(0, 0)
                step(1, 1)
                with act.Fori(0, (E - 4) // 2) as i:
                    step(0, 2 * i + 2)
                    step(1, 2 * i + 3)
                step(0, E - 2)
                for k in range(FK):
                    out_high(E - 1, k, last=True)
                out_half(1, E - 1)

                most_reg = act.value_load(most[0:1, 0:1], min_val=0, max_val=S)
                with act.If(most_reg > CAP):
                    for par in range(2):
                        act.wait_ge(y_st[par], 16 * (E // 2) + layer * 8 * E)
                    with act.Fori(0, (ROUNDS - 1) * E) as i:
                        act.wait_ge(o_pe[layer], 4 * i + 4 + 2)
                        a.activation(sgb[:, 0, :], ps[:, 0, :], ACT.Sigmoid).then_inc(o_sg[layer], 1)
                        act.wait_ge(o_dve[layer], 5 * i + 5)
                        dst = far_dram.rearrange("(e r n) d -> r e n d", r=ROUNDS, n=CAP)
                        dst = dst[bass.ds(i // E + 1, 1), bass.ds(i % E, 1)].rearrange("r e n d -> (r e n) d")
                        act.dma_start(dst, yo[0:CAP, 0, :]).then_inc(o_st[layer], 16)
                        act.wait_ge(o_st[layer], 16 * (i + 1))

            for layer in range(2):
                if layer == 1:
                    for u in range(UNITS_1, UNITS_1 + 4):
                        w_high(u)
                    act.wait_ge(cc_v, 1)
                    for j in range(KD):
                        if j < KD - 1:
                            w_high(UNITS_1 + 2 + 2 * (j + 1))
                        if j % 2 == 0:
                            mem_probs(1, j // 2)
                        for tap in range(PE_TAPS[j]):
                            k = TAPS_BEFORE[j] + tap
                            if k >= DIAGS:
                                act.wait_ge(cv_mm, k - DIAGS + 1)
                            a.activation(dg[:, k % DIAGS, :], ident[:, :], ACT.Copy, scale=convc[:, j, tap:tap + 1]).then_inc(dg_a, 1)
                        act.wait_ge(*gate_event(j))
                        if j >= 2:
                            act.wait_ge(gl_v, j - 1)
                        a.activation(gl[:, j % 2, :], ps[:, 2 * (j % 2) + 1, :], ACT.Sigmoid).then_inc(gl_a, 1)
                        if j < KD - 1:
                            w_high(UNITS_1 + 3 + 2 * (j + 1))
                    for ct in range(KD):
                        act.wait_ge(yc_v, ct + 1)
                        if ct >= 2:
                            act.wait_ge(var_mm, ct - 1)
                        a.activation(gl[:, ct % 2, :], mixT[:, ct, :], ACT.Square).then_inc(sq_a, 1)
                    act.wait_ge(var_v, 1)
                    a.activation(t0, rs_b, ACT.Ln).then_inc(lnv_a, 1)
                    act.wait_ge(lnv_a, 1)
                    a.activation(t0, t0, ACT.Exp, scale=-0.5).then_inc(lnv_a, 1)
                    for ct in range(KD):
                        act.wait_ge(z_g, ct + 1)
                        if ct >= 2:
                            act.wait_ge(mix_v, ct - 1)
                        a.activation(gl[:, ct % 2, :], mixT[:, ct, :], ACT.Sigmoid, scale=convc[:, ct, TAPS + 1:TAPS + 2],
                                     bias=convc[:, ct, TAPS + 2:TAPS + 3]).then_inc(su_a, 1)
                xT_half(layer)
                act.wait_ge(rt_mm, 1 + layer)
                a.activation(sc[:, :, :], ps[:, 0, 0:TT * E].rearrange("p (t e) -> p t e", e=E), ACT.Sigmoid).then_inc(sig_a, 1)
                moe(layer)
                if layer == 0:
                    x_high(1)

        @block.vector
        def _(dve):
            v_ = nc.vector
            own = Order(dve, v_order)

            def xT_half(layer, t):
                dve.wait_ge(tp_mm, (2 * layer + 1) * 2 * TT + 2 * t + 2)
                v_.tensor_copy(xT[:, 4:8, t * P:(t + 1) * P], ps[:, 5 + (t % 2) * 2, :].rearrange("p (k n) -> p k n", k=4)
                               ).then_inc(xT_v, 1)

            def x_low(layer, t):
                for b in range(2):
                    cols = slice(t * P, (t + 1) * P)
                    dve.wait_ge(xh_a, layer * 2 * TT + 2 * t + b + 1)
                    v_.tensor_tensor(xl[:, 4 * b:4 * b + 4, cols], ps[:, 4 + (t % 2) * 2 + b, :].rearrange("p (k n) -> p k n", k=4),
                                     xh[:, 4 * b:4 * b + 4, cols].bitcast(F32), ALU.subtract).then_inc(xl_v, 1)

            def w_low(u):
                dve.wait_ge(wh_a, u + 1)
                v_.tensor_tensor(wl[:, :, u % 2, :], unit_raw(u), wh[:, :, u % 2, :].bitcast(F32), ALU.subtract).then_inc(wl_v, 1)

            for t in range(TT):
                x_low(0, t)
            for m in range(MT):
                dve.wait_ge(mt_mm, 2 * m + 2)
                v_.tensor_copy(memT[:, 4:8, m * P:(m + 1) * P], ps[:, 1 + 2 * m, :].rearrange("p (k n) -> p k n", k=4)).then_inc(mt_v, 1)

            def mq_evac(j):
                dve.wait_ge(*mq_event(0, j))
                v_.tensor_copy(mqT[:, j, :], ps[:, j % 2, :]).then_inc(pj_ev, 1)

            w_low(0)
            w_low(1)
            dve.wait_ge(chunks_used, N_KV)
            def qkv_evac(g, i):
                j = 2 + 8 * g + i
                buf = g % 2
                dve.wait_ge(*proj_event(g, i))
                if g >= 2:
                    dve.wait_ge(av_mm, 2 * (g - 1))
                if i < 2:
                    ins = v_.tensor_scalar(qT[:, 2 * buf + i, :], ps[:, j % 2, :], float(P) ** -0.5, None, ALU.mult)
                elif i < 4:
                    ins = v_.tensor_copy(kT[:, 2 * buf + i - 2, :], ps[:, j % 2, :])
                else:
                    ins = v_.tensor_copy(v[:, TT * buf + i - 4, :], ps[:, j % 2, 0:COLS])
                ins.then_inc(pj_ev, 1)

            def head_soft(h, m=None):
                for r in range(TT):
                    kb = TT - 1 - r
                    o, n = blk(kb)
                    dve.wait_ge(z_mm, TT * h + r + 1)
                    if r >= 2:
                        dve.wait_ge(soft_v, TT * h + r - 1)
                    elif h:
                        dve.wait_ge(soft_v, TT * h)
                    v_.tensor_single_scalar(lt[:, r % 2, 0:n].bitcast(I32), ps[:, 2 + kb, 0:n].bitcast(I32), 0x7FFFFFFF,
                                            ALU.bitwise_and).then_inc(abs_v, 1)
                    if m is not None and r == 1:
                        mem_turned(0, m)
                    if r >= 1:
                        soft_out(h, r - 1)
                    if m is not None and r == TT - 1:
                        mem_out(0, m)
                soft_out(h, TT - 1)

            def soft_out(h, r):
                kb = TT - 1 - r
                o, n = blk(kb)
                dve.wait_ge(l_a, TT * h + r + 1)
                if h:
                    dve.wait_ge(c_mm, TT * h)
                v_.scalar_tensor_tensor(out=soft[:, o:o + n], in0=ps[:, 2 + kb, 0:n], scalar=0.0, in1=lt[:, r % 2, 0:n],
                                        op0=ALU.max, op1=ALU.add).then_inc(soft_v, 1)

            def head_out(h):
                dve.wait_ge(av_mm, h + 1)
                v_.tensor_copy(mixT[:, h, :], ps[:, 6 + h % 2, :]).then_inc(av_ev, 1)

            def mem_max(layer, h):
                dve.wait_ge(ms_mm, h + 1 + layer * MEM_HEADS)
                b = mem_bank[layer]
                own.mark(v_.tensor_reduce(mstat[:, 0, :], ps[:, b:b + 2, :].rearrange("p b (q m) -> p (b q) m", q=2), AX_X, ALU.max))
                own.wait()
                v_.tensor_scalar(mstat[:, 0, :], mstat[:, 0, :], -(MEM_DH ** -0.5), None, ALU.mult).then_inc(ms_v, 1)

            def mem_norm(layer, h):
                dve.wait_ge(ms_a, TT * (h + 1) + layer * MEM_HEADS * TT)
                own.mark(v_.reciprocal(mstat[:, 1, :], mstat[:, 1, :]))
                own.wait()
                v_.tensor_tensor(probs[:, :, :], probs[:, :, :], mstat[:, 1, :].unsqueeze(2).to_broadcast([P, TT, MEM]), ALU.mult
                                 ).then_inc(mp_v, 1)

            def mem_turned(layer, h):
                dve.wait_ge(mt2_mm, h + 1 + layer * MEM_HEADS)
                b = mem_bank[layer]
                v_.tensor_copy(pT[:, :, :], ps[:, b:b + 2, :]).then_inc(mt2_v, 1)

            def mem_out(layer, h):
                dve.wait_ge(mo_mm, h + 1 + layer * MEM_HEADS)
                o = MEM_DH * (h % 2)
                v_.tensor_copy(mixT[o:o + MEM_DH, KD + h // 2, :], ps[o:o + MEM_DH, mem_bank[layer], :]).then_inc(mo_v, 1)

            for j in range(2):
                mq_evac(j)
                w_low(2 + j)
            for i in range(8):
                qkv_evac(0, i)
                if i < 4:
                    w_low(4 + i)
            for g in range(3):
                for step in range(4):
                    h = 2 * g + step // 2
                    u = 8 + 6 * g + 2 * step
                    if step % 2 == 0:
                        w_low(u)
                        w_low(u + 1)
                        head_soft(h)
                    for i in range(2):
                        qkv_evac(g + 1, 2 * step + i)
                        if step == 0:
                            w_low(u + 2 + i)
                    if step % 2:
                        head_out(h)
            for h in range(HEADS - 2, HEADS):
                m = 2 * (h - HEADS + 2)
                if m == 0:
                    mem_max(0, m)
                    mem_norm(0, m)
                head_soft(h, m)
                mem_max(0, m + 1)
                mem_norm(0, m + 1)
                mem_turned(0, m + 1)
                mem_out(0, m + 1)
                if m == 0:
                    mem_max(0, m + 2)
                    mem_norm(0, m + 2)
                head_out(h)

            def norm_head(i, t):
                own.wait()
                for n in range(2):
                    own.mark(v_.bn_stats(stats[:, t, n, :], xrow[:, t, n * 512:(n + 1) * 512]))
                own.wait()
                own.mark(v_.bn_aggr(mv[:, t, :], stats[:, t, :, :].rearrange("p a b -> p (a b)")))
                own.wait()
                v_.tensor_scalar(mv[:, t, 1:2], mv[:, t, 1:2], LN_EPS, None, ALU.add).then_inc(ln_var, 1)

            def norm_mid(i, t):
                if t == 0:
                    dve.wait_ge(ln_in, 32 * (i + 1))
                own.mark(v_.scalar_tensor_tensor(out=xrow[:, t, :], in0=xrow[:, t, :], scalar=mv[:, t, 0:1], in1=lnp[:, 0, :],
                                                 op0=ALU.subtract, op1=ALU.mult))
                dve.wait_ge(ln_rs, i * TT + t + 1)
                own.wait()
                v_.scalar_tensor_tensor(out=xrow[:, t, :], in0=xrow[:, t, :], scalar=rstd[:, t:t + 1], in1=lnp[:, 1, :],
                                        op0=ALU.mult, op1=ALU.add).then_inc(row_ready, 1)

            def residual(layer):
                for t in range(TT):
                    for n in range(2):
                        j = 2 * t + n
                        dve.wait_ge(*out_event(layer, j))
                        cols = slice(n * 512, n * 512 + 512)
                        v_.scalar_tensor_tensor(out=xrow[:, t, cols], in0=xrow[:, t, cols], scalar=ALPHA, in1=ps[:, j % 4, :],
                                                op0=ALU.mult, op1=ALU.add).then_inc(op_v, 1)
                    dve.wait_ge(op_v, 2 * t + 2 + layer * 2 * TT)
                    norm_head(2 * layer, t)
                    norm_mid(2 * layer, t)
                    if t >= 2:
                        xT_half(layer, t - 2)
                xT_half(layer, TT - 2)
                xT_half(layer, TT - 1)

            def route(layer):
                def step(ins):
                    own.mark(ins)
                    own.wait()

                def best(vals, rank, onehot, n):
                    step(v_.tensor_reduce(top[:, :], vals, AX_X, ALU.max))
                    wide = top[:, :].unsqueeze(2).to_broadcast([P, TT, n])
                    key = ekey[:, :, 0:n]
                    step(v_.tensor_tensor(key, vals, wide, ALU.is_equal))
                    step(v_.tensor_tensor(key, key, rank, ALU.mult))
                    step(v_.tensor_reduce(top[:, :], key, AX_X, ALU.max))
                    step(v_.tensor_tensor(onehot, key, wide, ALU.is_equal))

                dve.wait_ge(small_in, 16 * (1 + TT))
                dve.wait_ge(consts2, 9)
                dve.wait_ge(sig_a, 1 + layer)
                step(v_.tensor_tensor(scb[:, :, :], sc[:, :, :], rb[:, :, :], ALU.add))
                by4 = scb[:, :, :].rearrange("p t (g e) -> p (t g) e", e=PER_GROUP)
                own.mark(v_.tensor_tensor(pair[:, :, 0:3], by4[:, :, 0:3], by4[:, :, 1:4], ALU.add))
                own.mark(v_.tensor_tensor(pair[:, :, 3:5], by4[:, :, 0:2], by4[:, :, 2:4], ALU.add))
                step(v_.tensor_tensor(pair[:, :, 5:6], by4[:, :, 0:1], by4[:, :, 3:4], ALU.add))
                step(v_.tensor_reduce(gs[:, :, :].rearrange("p t g -> p (t g)"), pair[:, :, :], AX_X, ALU.max))
                best(gs[:, :, :], rank_g[:, :, :], ge[:, :, :], GROUPS)
                step(v_.tensor_scalar(ge[:, :, :], ge[:, :, :], 1.0, BIG, ALU.subtract, ALU.mult))
                step(v_.tensor_tensor(by4, by4, ge[:, :, :].rearrange("p t g -> p (t g)").unsqueeze(2)
                                      .to_broadcast([P, TT * GROUPS, PER_GROUP]), ALU.add))
                best(scb[:, :, :], rank_e[:, :, :], oh1[:, :, :], E)
                step(v_.scalar_tensor_tensor(out=scb[:, :, :], in0=oh1[:, :, :], scalar=-4.0 * BIG, in1=scb[:, :, :],
                                             op0=ALU.mult, op1=ALU.add))
                best(scb[:, :, :], rank_e[:, :, :], oh2[:, :, :], E)
                v_.tensor_tensor(both[:, 0:TT, :], oh1[:, :, :], oh2[:, :, :], ALU.add).then_inc(pick_v, 1)
                dve.wait_ge(pos_mm, 1 + layer)
                pos = ps[:, 5, 0:TT * E].rearrange("p (t e) -> p t e", e=E)
                step(v_.scalar_tensor_tensor(out=place[:, :, :], in0=pos, scalar=1.0, in1=both[:, 0:TT, :], op0=ALU.add, op1=ALU.mult))

            def match_tokens(where, of, group):
                experts = of[:, :, group * PER_TABLE:(group + 1) * PER_TABLE]
                return v_.tensor_tensor(where, one_up[:, :].unsqueeze(1).unsqueeze(1).to_broadcast([P, TT, PER_TABLE, CAP]),
                                        experts.unsqueeze(3).to_broadcast([P, TT, PER_TABLE, CAP]), ALU.is_equal)

            def table(layer, group):
                done = group + TABLES * layer
                if group >= 2:
                    dve.wait_ge(tab_mm, done - 1)
                match_tokens(match[:, group % 2], place, group).then_inc(match_v, 1)
                dve.wait_ge(tab_mm, done + 1)
                e0 = group * PER_TABLE
                v_.tensor_reduce(tok_f[0:CAP, e0:e0 + PER_TABLE], ps[0:CAP, 5, 128 + 2 * e0:128 + 2 * e0 + 2 * PER_TABLE]
                                 .rearrange("p (e a) -> p e a", a=2), AX_X, ALU.add).then_inc(tok_v, 1)
                dve.wait_ge(tok_v, done + 1)
                v_.tensor_copy(slot_tok[0:CAP, 0, e0:e0 + PER_TABLE], tok_f[0:CAP, e0:e0 + PER_TABLE]).then_inc(slot_tok_v, 1)

            def slots_and_gates(layer):
                def step(ins):
                    own.mark(ins)
                    own.wait()

                for k, oh in enumerate((oh1, oh2)):
                    step(v_.tensor_tensor(ekey[:, :, :], sc[:, :, :], oh[:, :, :], ALU.mult))
                    step(v_.tensor_reduce(gate[:, k, :], ekey[:, :, :], AX_X, ALU.add))
                step(v_.tensor_tensor(gsum[:, :], gate[:, 0, :], gate[:, 1, :], ALU.add))
                step(v_.reciprocal(gsum[:, :], gsum[:, :]))
                for k in range(2):
                    step(v_.tensor_tensor(gate[:, k, :], gate[:, k, :], gsum[:, :], ALU.mult))
                pos = ps[:, 5, 0:TT * E].rearrange("p (t e) -> p t e", e=E)
                step(v_.tensor_tensor(scb[:, :, :], pos, seg_base[:, :, :], ALU.add))
                for k, oh in enumerate((oh1, oh2)):
                    step(v_.tensor_tensor(ekey[:, :, :], scb[:, :, :], oh[:, :, :], ALU.mult))
                    step(v_.tensor_reduce(slot_f[:, k, :], ekey[:, :, :], AX_X, ALU.add))
                v_.tensor_copy(slot_i[:, :, :], slot_f[:, :, :]).then_inc(slots_v, 1)
                step(v_.tensor_reduce(most_f[:, :], ps[:, 5, TT * E:TT * E + E], AX_X, ALU.max))
                v_.tensor_copy(most[:, :], most_f[:, :]).then_inc(slots_v, 1)
                step(v_.tensor_scalar(scb[:, :, :], pos, float(CAP), float(2 * E * S), ALU.is_ge, ALU.mult))
                step(v_.tensor_tensor(scb[:, :, :], scb[:, :, :], near_base[:, :, :], ALU.add))
                step(v_.tensor_tensor(scb[:, :, :], scb[:, :, :], pos, ALU.add))
                for k, oh in enumerate((oh1, oh2)):
                    step(v_.tensor_tensor(ekey[:, :, :], scb[:, :, :], oh[:, :, :], ALU.mult))
                    step(v_.tensor_reduce(near_f[:, k, :], ekey[:, :, :], AX_X, ALU.add))
                step(v_.tensor_scalar(near_gate[:, :, :], near_f[:, :, :], float(E * S), None, ALU.is_lt))
                step(v_.tensor_tensor(near_f[:, :, :], near_f[:, :, :], near_gate[:, :, :], ALU.mult))
                step(v_.tensor_copy(near_i[:, :, :], near_f[:, :, :]))
                step(v_.tensor_tensor(near_gate[:, :, :], near_gate[:, :, :], gate[:, :, :], ALU.mult))

            def moe(layer):
                def half1(par, e):
                    dve.wait_ge(xt_mm, 2 * e + 2 + layer * 2 * E)
                    v_.tensor_copy(xgT[:, par, 4:8, :], ps[:, 6, :].rearrange("p (k n) -> p k n", k=4)).then_inc(xt_v, 1)

                def activate(par, e):
                    dve.wait_ge(sg_a, e + 1 + layer * E)
                    v_.tensor_tensor(hact[:, par, :], hact[:, par, :], ps[:, 2 * par, :], ALU.mult).then_inc(sg_v, 1)
                    dve.wait_ge(sg_v, e + 1 + layer * E)
                    v_.tensor_tensor(hact[:, par, :], hact[:, par, :], ps[:, 2 * par + 1, :], ALU.mult).then_inc(h_v, 1)

                def hT_evac(par, e):
                    dve.wait_ge(ht_mm, e + 1 + layer * E)
                    turned = ps[:, 6, :].rearrange("p (k n) -> p k n", k=4)
                    v_.tensor_copy(hTh[:, par, :, :], turned).then_inc(hTh_v, 1)
                    dve.wait_ge(hTh_v, e + 1 + layer * E)
                    v_.tensor_tensor(hTl[:, par, :, :], turned, hTh[:, par, :, :].bitcast(F32), ALU.subtract).then_inc(ht_v, 1)

                def out_low(e, k, last=False):
                    n = (BASE_MOE[layer] + E * STEP - CB if last else BASE_MOE[layer] + 2 * CA) + k // PIECE
                    dve.wait_ge(out_h_a, FK * e + k + 1 + layer * FK * E)
                    v_.tensor_tensor(out_l[k], ring_rows(n)[:, k % PIECE, :], out_h[k].bitcast(F32), ALU.subtract).then_inc(out_l_v, 1)

                def out_half(par, e):
                    dve.wait_ge(chunks_used, second_done(BASE_MOE[layer], e))
                    if not isinstance(e, int) or e > 1:
                        dve.wait_ge(y_st[par], 8 * (e - par) + layer * 8 * E)
                    v_.tensor_copy(yo[:, par, 512:1024], ps[:, 5, :]).then_inc(y_v, 1)

                def step(par, s):
                    hT_evac(par, s)
                    out_low(s, 0)
                    out_low(s, 1)
                    activate(1 - par, s + 1)
                    out_low(s, 2)
                    out_low(s, 3)
                    if not isinstance(s, int) or s < E - 2:
                        half1(par, s + 2)
                    out_half(par, s)

                half1(0, 0)
                for group in range(2, TABLES):
                    table(layer, group)
                slots_and_gates(layer)
                activate(0, 0)
                half1(1, 1)
                step(0, 0)
                dve.wait_ge(rows_out, 16 * TT * (layer + 1))
                for t in range(TT):
                    own.mark(v_.tensor_scalar(xrow[:, t, :], xrow[:, t, :], ALPHA, None, ALU.mult))
                own.wait()
                step(1, 1)
                with dve.Fori(0, (E - 4) // 2) as i:
                    step(0, 2 * i + 2)
                    step(1, 2 * i + 3)
                step(0, E - 2)
                hT_evac(1, E - 1)
                for k in range(FK):
                    out_low(E - 1, k, last=True)
                out_half(1, E - 1)

                most_reg = dve.value_load(most[0:1, 0:1], min_val=0, max_val=S)
                with dve.If(most_reg > CAP):
                    for par in range(2):
                        dve.wait_ge(y_st[par], 16 * (E // 2) + layer * 8 * E)
                    for r in range(1, ROUNDS):
                        before_r = (3 + TABLES) * (r - 1)
                        v_.tensor_scalar(ekey[:, :, :], place[:, :, :], float(r * CAP), None, ALU.subtract).then_inc(o_match[layer], 1)
                        dve.wait_ge(o_match[layer], before_r + 1)
                        for group in range(TABLES):
                            if r > 1 or group:
                                dve.wait_ge(o_tab[layer], TABLES * (r - 1) + group)
                            match_tokens(match[:, 0], ekey, group).then_inc(o_match[layer], 1)
                        dve.wait_ge(o_tab[layer], TABLES * r)
                        v_.tensor_reduce(tok_f[0:CAP, :], ps[0:CAP, 5, 128:128 + 2 * E].rearrange("p (e a) -> p e a", a=2),
                                         AX_X, ALU.add).then_inc(o_match[layer], 1)
                        dve.wait_ge(o_match[layer], before_r + TABLES + 2)
                        v_.tensor_copy(slot_tok[0:CAP, r, :], tok_f[0:CAP, :]).then_inc(o_match[layer], 1)
                    with dve.Fori(0, (ROUNDS - 1) * E) as i:
                        dve.wait_ge(o_pe[layer], 4 * i + 4 + 1)
                        v_.tensor_copy(xgT[:, 0, :, :], ps[:, 6:8, :].rearrange("p b (k n) -> p (b k) n", k=4)).then_inc(o_dve[layer], 1)
                        dve.wait_ge(o_sg[layer], i + 1)
                        v_.tensor_tensor(hact[:, 0, :], hact[:, 0, :], ps[:, 0, :], ALU.mult).then_inc(o_dve[layer], 1)
                        dve.wait_ge(o_dve[layer], 5 * i + 2)
                        v_.tensor_tensor(hact[:, 0, :], hact[:, 0, :], ps[:, 1, :], ALU.mult).then_inc(o_dve[layer], 1)
                        dve.wait_ge(o_pe[layer], 4 * i + 4 + 3)
                        v_.tensor_copy(hT[:, 0, :, :], ps[:, 2, :].rearrange("p (k n) -> p k n", k=4)).then_inc(o_dve[layer], 1)
                        dve.wait_ge(o_pe[layer], 4 * i + 4 + 4)
                        v_.tensor_copy(yo[:, 0, :], ps[:, 4:6, :].rearrange("p b n -> p (b n)")).then_inc(o_dve[layer], 1)
                    v_.tensor_tensor(far_gate[:, :, :], gate[:, :, :], near_gate[:, :, :], ALU.subtract).then_inc(o_dve[layer], 1)
                    dve.wait_ge(o_dve[layer], FAR_DVE)
                    for t in range(TT):
                        for k in range(2):
                            dve.wait_ge(o_far[layer][k], 16 * (t + 1))
                            v_.scalar_tensor_tensor(out=xrow[:, t, :], in0=yg[:, k, :], scalar=far_gate[:, k, t:t + 1], in1=xrow[:, t, :],
                                                    op0=ALU.mult, op1=ALU.add).then_inc(o_dve[layer], 1)
                            dve.wait_ge(o_dve[layer], FAR_DVE + 2 * t + k + 1)

            def combine(layer):
                i = 2 * layer + 1
                for t in range(TT):
                    for k in range(2):
                        dve.wait_ge(yg_in[2 * t + k], 16 * (layer + 1))
                        v_.scalar_tensor_tensor(out=xrow[:, t, :], in0=yg[:, 2 * t + k, :], scalar=near_gate[:, k, t:t + 1],
                                                in1=xrow[:, t, :], op0=ALU.mult, op1=ALU.add).then_inc(yg_v, 1)
                        dve.wait_ge(yg_v, 2 * t + k + 1 + layer * 2 * TT)
                    norm_head(i, t)
                    norm_mid(i, t)
                    if layer == 0 and t >= 2:
                        x_low(1, t - 2)

            def conv_taps(ct, first, last):
                for tap in range(first, last):
                    if tap > PE_TAPS[ct] + 1:
                        dve.wait_ge(v_order, own.n - 1)
                    src, weight = hpad[:, ct, 2 + tap:2 + tap + S], convc[:, ct, tap:tap + 1]
                    total = t0 if (tap - PE_TAPS[ct]) % 2 else mixT[:, ct, :]
                    if tap == PE_TAPS[ct]:
                        own.mark(v_.tensor_scalar(total, src, weight, convc[:, ct, TAPS:TAPS + 1], ALU.mult, ALU.add))
                    elif tap == PE_TAPS[ct] + 1:
                        own.mark(v_.tensor_scalar(total, src, weight, None, ALU.mult))
                    else:
                        own.mark(v_.scalar_tensor_tensor(out=total, in0=src, scalar=weight, in1=total, op0=ALU.mult, op1=ALU.add))
                if last == TAPS:
                    own.wait()
                    own.mark(v_.tensor_tensor(mixT[:, ct, :], mixT[:, ct, :], t0, ALU.add))
                    dve.wait_ge(cv_mm, TAPS_BEFORE[ct + 1])
                    own.wait()
                    v_.tensor_tensor(mixT[:, ct, :], mixT[:, ct, :], ps[:, 6 + ct % 2, :], ALU.add).then_inc(cv_v, 1)
                    dve.wait_ge(cv_v, ct + 1)

            def conv_layer():
                dve.wait_ge(pad_g, 1)
                for j in range(2):
                    dve.wait_ge(*mq_event(1, j))
                    v_.tensor_copy(mqT[:, j, :], ps[:, 4 + j, :]).then_inc(mq_v, 1)
                dve.wait_ge(cc_mm, 2)
                v_.tensor_copy(convc[:, :, :], ps[:, 6:8, :].rearrange("p b (k n) -> p (b k) n", n=P)[:, :, 0:TAPS + 3]).then_inc(cc_v, 1)
                dve.wait_ge(cc_v, 1)
                mem_max(1, 0)
                mem_norm(1, 0)
                for j in range(KD):
                    dve.wait_ge(*gate_event(j))
                    dve.wait_ge(gl_a, j + 1)
                    v_.tensor_tensor(hpad[:, j, 32:32 + S], gl[:, j % 2, :], ps[:, 2 * (j % 2), :], ALU.mult).then_inc(gl_v, 1)
                    dve.wait_ge(gl_v, j + 1)
                    mid = (PE_TAPS[j] + TAPS) // 2
                    if j % 2:
                        mem_out(1, j // 2)
                    conv_taps(j, PE_TAPS[j], mid)
                    if j % 2 == 0:
                        mem_turned(1, j // 2)
                    elif j < KD - 1:
                        mem_max(1, j // 2 + 1)
                    conv_taps(j, mid, TAPS)
                    if j % 2 and j < KD - 1:
                        mem_norm(1, j // 2 + 1)
                dve.wait_ge(mu_mm, 1)
                v_.tensor_scalar(mean_b, ps[:, 0, :], 1.0 / D, None, ALU.mult).then_inc(mu_v, 1)
                dve.wait_ge(mu_v, 1)
                for ct in range(KD):
                    v_.tensor_tensor(mixT[:, ct, :], mixT[:, ct, :], mean_b, ALU.subtract).then_inc(yc_v, 1)
                dve.wait_ge(var_mm, KD)
                v_.tensor_scalar(rs_b, ps[:, 3, :], 1.0 / D, LN_EPS, ALU.mult, ALU.add).then_inc(var_v, 1)
                dve.wait_ge(lnv_a, 2)
                own.mark(v_.tensor_tensor(t1, t0, t0, ALU.mult))
                own.wait()
                own.mark(v_.tensor_tensor(t1, t1, rs_b, ALU.mult))
                own.wait()
                own.mark(v_.tensor_scalar(t1, t1, -0.5, 1.5, ALU.mult, ALU.add))
                own.wait()
                v_.tensor_tensor(rs_b, t1, t0, ALU.mult).then_inc(rsb_v, 1)
                dve.wait_ge(rsb_v, 1)
                for ct in range(KD):
                    u = (t0, t1)[ct % 2]
                    dve.wait_ge(z_g, ct + 1)
                    own.mark(v_.tensor_scalar(u, mixT[:, ct, :], convc[:, ct, TAPS + 1:TAPS + 2], convc[:, ct, TAPS + 2:TAPS + 3],
                                              ALU.mult, ALU.add))
                    dve.wait_ge(su_a, ct + 1)
                    own.wait()
                    v_.tensor_tensor(mixT[:, ct, :], u, gl[:, ct % 2, :], ALU.mult).then_inc(mix_v, 1)
                    dve.wait_ge(mix_v, ct + 1)

            for layer in range(2):
                if layer == 1:
                    conv_layer()
                residual(layer)
                route(layer)
                table(layer, 0)
                table(layer, 1)
                moe(layer)
                combine(layer)
                if layer == 0:
                    x_low(1, TT - 2)
                    x_low(1, TT - 1)

        @block.tensor
        def _(pe):
            t_ = nc.tensor

            def x_transpose(i, t):
                if i:
                    pe.wait_ge(row_ready, (i - 1) * TT + t + 1)
                if t >= 2 and i % 2:
                    pe.wait_ge(xT_a, (i // 2) * TT + t - 1)
                    pe.wait_ge(xT_v, (i // 2) * TT + t - 1)
                elif t >= 2:
                    pe.wait_ge(xl_v, (i // 2) * 2 * TT + 2 * t - 2)
                for b in range(2):
                    for k in range(4):
                        ins = t_.transpose(ps[:, 4 + (t % 2) * 2 + b, k * P:(k + 1) * P],
                                           xrow[:, t, (4 * b + k) * P:(4 * b + k + 1) * P], ident[:, :])
                    ins.then_inc(tp_mm, 1)

            pe.wait_ge(consts, 6)
            pe.wait_ge(x_in, 16 * TT)
            for t in range(TT):
                x_transpose(0, t)
            pe.wait_ge(mem_in, 16)
            for m in range(MT):
                for b in range(2):
                    for k in range(4):
                        ins = t_.transpose(ps[:, 2 * m + b, k * P:(k + 1) * P],
                                           memrow[:, m, (4 * b + k) * P:(4 * b + k + 1) * P], ident[:, :])
                    ins.then_inc(mt_mm, 1)
            pe.wait_ge(mt_a, MT)
            pe.wait_ge(mt_v, MT)

            for j in range(8):
                layer, kind, i = j // 4, (j // 2) % 2, j % 2
                n = 2 * layer + kind
                pe.wait_ge(landed[slot_of(n)], loaded(n))
                if j >= 2:
                    pe.wait_ge(kv_ev, j - 1)
                elif j == 0:
                    pe.wait_ge(xl_v, 2 * TT)
                w = ring_cols(n)
                for k in range(KD):
                    if kind == 0:
                        ins = t_.matmul(ps[:, 4 + j % 2, 0:MEM], w[:, k, i * P:(i + 1) * P], memT[:, k, :],
                                        start=(k == 0), stop=(k == KD - 1))
                    else:
                        ins = t_.matmul(ps[:, 4 + j % 2, 0:MEM], memT[:, k, i * P:(i + 1) * P], w[:, k, :],
                                        start=(k == 0), stop=(k == KD - 1))
                ins.then_inc(kv_event(j)[0], 1)

            def split_matmuls(dst, hi, lo, moving_hi, moving_lo, first, last):
                t_.matmul(dst, hi, moving_hi, start=first, stop=False)
                t_.matmul(dst, lo, moving_hi, start=False, stop=False)
                return t_.matmul(dst, hi, moving_lo, start=False, stop=last)

            def unit_ready(u):
                if u < UNITS_1:
                    pe.wait_ge(wl_v, u + 1)
                else:
                    pe.wait_ge(wl_g, u + 1 - UNITS_1)
                pe.wait_ge(wh_a, u + 1)

            def feature_tile(bank, u):
                unit_ready(u)
                for k in range(KD):
                    ins = split_matmuls(ps[:, bank, :], wh[:, k, u % 2, :], wl[:, k, u % 2, :], xh[:, k, :], xl[:, k, :],
                                        k == 0, k == KD - 1)
                return ins

            for j in range(2):
                feature_tile(j, j).then_inc(mq_event(0, j)[0], 1)

            def project(g, i):
                j = 2 + 8 * g + i
                u = 2 + 6 * g + min(i, 4)
                pe.wait_ge(pj_ev, j - 1)
                if i < 4:
                    ins = feature_tile(j % 2, u)
                else:
                    unit_ready(u + 1)
                    rows = slice((i - 4) * P, (i - 3) * P)
                    for k in range(KD):
                        ins = split_matmuls(ps[:, j % 2, 0:COLS].rearrange("p (i n) -> p i n", i=2), xh[:, k, rows], xl[:, k, rows],
                                            wh[:, k, :, :], wl[:, k, :, :], k == 0, k == KD - 1)
                ins.then_inc(proj_event(g, i)[0], 1)

            def scores(h):
                buf = 2 * ((h // 2) % 2) + h % 2
                pe.wait_ge(pj_ev, 2 + 8 * (h // 2 + 1))
                if h == 0:
                    pe.wait_ge(kv_ev, 8)
                for r in range(TT):
                    kb = TT - 1 - r
                    n = blk(kb)[1]
                    if h:
                        pe.wait_ge(w_a, TT * (h - 1) + r + 1)
                    t_.matmul(ps[:, 2 + kb, 0:n], kT[:, buf, kb * P:(kb + 1) * P], qT[:, buf, kb * P:S],
                              start=True, stop=True).then_inc(z_mm, 1)

            def later_sums(h):
                for r in range(TT):
                    kb = TT - 1 - r
                    pe.wait_ge(soft_g, TT * h + r + 1)
                    pe.wait_ge(soft_v, TT * h + r + 1)
                    for other in range(TT - 1, kb - 1, -1):
                        o, n = blk(other)
                        at = (other - kb) * P
                        ins = t_.matmul(ps[:, 2 + kb, at:at + n], (neg_tri if other == kb else neg_one)[:, :], soft[:, o:o + n],
                                        start=False, stop=True, skip_group_check=True)
                    ins.then_inc(c_mm, 1)

            def weigh(h):
                g, i = h // 2, h % 2
                if h >= 2:
                    pe.wait_ge(av_ev, h - 1)
                pe.wait_ge(w_g, TT * (h + 1))
                pe.wait_ge(w_a, TT * (h + 1))
                for kb in range(TT):
                    o, n = blk(kb)
                    ins = t_.matmul(ps[:, 6 + i, kb * P:S], v[:, TT * (g % 2) + kb, i * P:(i + 1) * P], aT[:, o:o + n],
                                    start=(kb == 0), stop=(kb == TT - 1))
                ins.then_inc(av_mm, 1)

            for i in range(8):
                project(0, i)
            def mem_scores(layer, h):
                hp, o = h // 2, MEM_DH * (h % 2)
                if h:
                    pe.wait_ge(mo_v, h + layer * MEM_HEADS)
                for q in range(TT):
                    ins = t_.matmul(ps[:, mem_bank[layer] + q // 2, (q % 2) * MEM:(q % 2) * MEM + MEM],
                                    mqT[o:o + MEM_DH, hp, q * P:(q + 1) * P], kTm[o:o + MEM_DH, layer, hp, :],
                                    start=True, stop=True)
                ins.then_inc(ms_mm, 1)

            def mem_turn(layer, h):
                pe.wait_ge(mp_v, h + 1 + layer * MEM_HEADS)
                for q in range(TT):
                    for m in range(MT):
                        ins = t_.transpose(ps[:, mem_bank[layer] + m, q * P:(q + 1) * P], probs[:, q, m * P:(m + 1) * P], ident[:, :])
                ins.then_inc(mt2_mm, 1)

            def mem_weigh(layer, h):
                o = MEM_DH * (h % 2)
                pe.wait_ge(mt2_v, h + 1 + layer * MEM_HEADS)
                for m in range(MT):
                    ins = t_.matmul(ps[o:o + MEM_DH, mem_bank[layer], :], vm[:, layer, m, h * MEM_DH:(h + 1) * MEM_DH],
                                    pT[:, m, :], start=(m == 0), stop=(m == MT - 1))
                ins.then_inc(mo_mm, 1)

            for g in range(3):
                for step in range(4):
                    h = 2 * g + step // 2
                    if step % 2 == 0:
                        scores(h)
                    project(g + 1, 2 * step)
                    project(g + 1, 2 * step + 1)
                    if step % 2 == 0:
                        later_sums(h)
                    else:
                        weigh(h)
            pe.wait_ge(pj_ev, 2 + 8 * 4)
            mem_scores(0, 0)
            for h in range(HEADS - 2, HEADS):
                m = 2 * (h - HEADS + 2)
                scores(h)
                mem_turn(0, m)
                mem_weigh(0, m)
                mem_scores(0, m + 1)
                later_sums(h)
                mem_turn(0, m + 1)
                mem_weigh(0, m + 1)
                if m == 0:
                    mem_scores(0, m + 2)
                weigh(h)

            def out_project(layer):
                for i, k in enumerate(MIX_ORDER):
                    c = BASE_WO[layer] + i // PIECE
                    if i % PIECE == 0:
                        pe.wait_ge(landed[slot_of(c)], loaded(c))
                    if i == MEM_TILES:
                        if layer == 0:
                            pe.wait_ge(av_ev, HEADS)
                    if i >= MEM_TILES and layer == 1:
                        pe.wait_ge(mix_v, k + 1)
                    for j in range(4):
                        t, n = j // 2, j % 2
                        ins = t_.matmul(ps[:, j, :], mixT[:, k, t * P:(t + 1) * P], ring_rows(c)[:, i % PIECE, n * 512:(n + 1) * 512],
                                        start=(i == 0), stop=(i == MIX_TILES - 1))
                        if i == MIX_TILES - 1:
                            ins.then_inc(op_mm, 1)
                for t in range(2, TT):
                    for n in range(2):
                        j = 2 * t + n
                        pe.wait_ge(op_v, j - 3 + layer * 2 * TT)
                        for i, k in enumerate(MIX_ORDER):
                            c = BASE_WO[layer] + i // PIECE
                            ins = t_.matmul(ps[:, j % 4, :], mixT[:, k, t * P:(t + 1) * P], ring_rows(c)[:, i % PIECE, n * 512:(n + 1) * 512],
                                            start=(i == 0), stop=(i == MIX_TILES - 1))
                        if j < 2 * TT - 1:
                            ins.then_inc(op_mm, 1)
                        else:
                            ins.then_inc(chunks_used, CW)
                    x_transpose(2 * layer + 1, t - 2)
                x_transpose(2 * layer + 1, TT - 2)

            def route(layer):
                pe.wait_ge(op_v, layer * 2 * TT + 5)
                for t in range(TT):
                    if t == TT - 1:
                        x_transpose(2 * layer + 1, t)
                    pe.wait_ge(xT_a, layer * TT + t + 1)
                    pe.wait_ge(xT_v, layer * TT + t + 1)
                    for k in range(KD):
                        ins = t_.matmul(ps[:, 0, t * E:(t + 1) * E], xT[:, k, t * P:(t + 1) * P], rw[:, k, :],
                                        start=(k == 0), stop=(k == KD - 1))
                ins.then_inc(rt_mm, 1)
                pe.wait_ge(pick_v, 1 + layer)
                t_.matmul(ps[:, 5, 0:(TT + 1) * E], before[:, :], both[:, :, :], start=True, stop=False, skip_group_check=True)
                for u in range(TT):
                    ins = t_.matmul(ps[:, 5, (u + 1) * E:(TT + 1) * E], ones_b[:, :], both[:, u, :].unsqueeze(1).to_broadcast([P, TT - u, E]),
                                    start=False, stop=True, skip_group_check=True)
                ins.then_inc(pos_mm, 1)

            def token_sums(where, group):
                for e in range(PER_TABLE):
                    for t in range(TT):
                        at = 128 + 2 * (group * PER_TABLE + e)
                        ins = t_.matmul(ps[0:CAP, 5, at:at + 2], where[:, t, e, :], tok_id[:, t, :], start=(t == 0), stop=(t == TT - 1))
                return ins

            def table(layer, group):
                pe.wait_ge(match_v, group + 1 + TABLES * layer)
                token_sums(match[:, group % 2], group).then_inc(tab_mm, 1)

            def moe(layer):
                base = BASE_MOE[layer]

                def rows_transpose(par, e, half):
                    if half == 0:
                        pe.wait_ge(gat[par], 8 * (e - par) + 16 + layer * 8 * E)
                        if not isinstance(e, int) or e > 0:
                            pe.wait_ge(xt_a, e + layer * E)
                    else:
                        if not isinstance(e, int) or e > 0:
                            pe.wait_ge(xt_v, e + layer * E)
                        if not isinstance(e, int) or e > 1:
                            pe.wait_ge(ht_v, e - 1 + layer * E)
                    bank = 7 - half
                    for k in range(4):
                        ins = t_.transpose(ps[:, bank, k * P:k * P + CAP], xg[0:CAP, par, (4 * half + k) * P:(4 * half + k + 1) * P],
                                           ident[0:CAP, 0:CAP])
                    ins.then_inc(xt_mm, 1)

                def first_product(par, e, n0, s, c):
                    n = n0 + c
                    pe.wait_ge(landed[slot_of(n)], 16 * s + loaded(n))
                    if c == 0:
                        if isinstance(e, int) and e == 0:
                            pe.wait_ge(sig_a, 1 + layer)
                        pe.wait_ge(xt_a, e + 1 + layer * E)
                        pe.wait_ge(xt_v, e + 1 + layer * E)
                        if not isinstance(e, int) or e > 1:
                            pe.wait_ge(h_v, e - 1 + layer * E)
                    w = ring_rows(n)
                    for k in range(PIECE):
                        for half in range(2):
                            kk = PIECE * c + k
                            ins = t_.matmul(ps[0:CAP, 2 * par + half, :], xgT[:, par, kk, :], w[:, k, half * 512:(half + 1) * 512],
                                            start=(kk == 0), stop=(kk == KD - 1))
                    ins.then_inc(chunks_used, 1)

                def h_transpose(par, e):
                    pe.wait_ge(h_v, e + 1 + layer * E)
                    if not isinstance(e, int) or e < E - 1:
                        pe.wait_ge(xt_v, e + 2 + layer * E)
                    for k in range(FK):
                        ins = t_.transpose(ps[:, 6, k * P:k * P + CAP], hact[0:CAP, par, k * P:(k + 1) * P], ident[0:CAP, 0:CAP])
                    ins.then_inc(ht_mm, 1)

                def second_product(par, e):
                    pe.wait_ge(ht_v, e + 1 + layer * E)
                    if not isinstance(e, int) or e > 0:
                        pe.wait_ge(y_a, e + layer * E)
                        pe.wait_ge(y_v, e + layer * E)
                    for c in range(CB):
                        for k in range(PIECE):
                            kk = PIECE * c + k
                            pe.wait_ge(out_l_v, FK * e + kk + 1 + layer * FK * E)
                            for half in range(2):
                                cols = slice(half * 512, (half + 1) * 512)
                                ins = split_matmuls(ps[0:CAP, 4 + half, :], hTh[:, par, kk, :], hTl[:, par, kk, :],
                                                    out_h[kk][:, cols], out_l[kk][:, cols], kk == 0, kk == FK - 1)
                        ins.then_inc(chunks_used, 1)

                def step(par, s):
                    n0 = base + CA
                    for c in range(CA):
                        first_product(1 - par, s + 1, n0, s, c)
                        if c == 0:
                            h_transpose(par, s)
                    if not isinstance(s, int) or s < E - 2:
                        rows_transpose(par, s + 2, 0)
                        rows_transpose(par, s + 2, 1)
                    second_product(par, s)

                table(layer, 0)
                table(layer, 1)
                rows_transpose(0, 0, 0)
                rows_transpose(0, 0, 1)
                for c in range(CA):
                    first_product(0, 0, base, 0, c)
                    if c < TABLES - 2:
                        table(layer, c + 2)
                rows_transpose(1, 1, 0)
                rows_transpose(1, 1, 1)
                step(0, 0)
                step(1, 1)
                with pe.Fori(0, (E - 4) // 2) as i:
                    step(0, 2 * i + 2)
                    step(1, 2 * i + 3)
                step(0, E - 2)
                h_transpose(1, E - 1)
                second_product(1, E - 1)

                most_reg = pe.value_load(most[0:1, 0:1], min_val=0, max_val=S)
                with pe.If(most_reg > CAP):
                    pe.wait_ge(y_a, E + layer * E)
                    pe.wait_ge(y_v, E + layer * E)
                    for i in range((ROUNDS - 1) * TABLES):
                        pe.wait_ge(o_match[layer], (3 + TABLES) * (i // TABLES) + 2 + i % TABLES)
                        token_sums(match[:, 0], i % TABLES).then_inc(o_tab[layer], 1)
                    pe.nop().then_inc(o_pe[layer], 4)
                    with pe.Fori(0, (ROUNDS - 1) * E) as i:
                        pe.wait_ge(o_x[layer], 16 * i + 16)
                        for k in range(KD):
                            ins = t_.transpose(ps[:, 6 + k // 4, (k % 4) * P:(k % 4) * P + CAP], xg[0:CAP, 0, k * P:(k + 1) * P],
                                               ident[0:CAP, 0:CAP])
                        ins.then_inc(o_pe[layer], 1)
                        pe.wait_ge(o_dve[layer], 5 * i + 1)
                        pe.wait_ge(o_w[layer], 16 * STEP * i + 16 * STEP)
                        for k in range(KD):
                            for half in range(2):
                                ins = t_.matmul(ps[0:CAP, half, :], xgT[:, 0, k, :], ring_rows(k // PIECE)[:, k % PIECE, half * 512:half * 512 + 512],
                                                start=(k == 0), stop=(k == KD - 1))
                        ins.then_inc(o_pe[layer], 1)
                        pe.wait_ge(o_dve[layer], 5 * i + 3)
                        for k in range(FK):
                            ins = t_.transpose(ps[:, 2, k * P:k * P + CAP], hact[0:CAP, 0, k * P:(k + 1) * P], ident[0:CAP, 0:CAP])
                        ins.then_inc(o_pe[layer], 1)
                        pe.wait_ge(o_dve[layer], 5 * i + 4)
                        for k in range(FK):
                            for half in range(2):
                                ins = t_.matmul(ps[0:CAP, 4 + half, :], hT[:, 0, k, :],
                                                ring_rows(CA + k // PIECE)[:, k % PIECE, half * 512:half * 512 + 512],
                                                start=(k == 0), stop=(k == FK - 1))
                        ins.then_inc(o_pe[layer], 1)

            def convolution():
                for j in range(2):
                    feature_tile(4 + j, UNITS_1 + j).then_inc(mq_event(1, j)[0], 1)
                pe.wait_ge(conv_in, 16 * 4)
                rows = TAPS + 3
                for k in range(KD):
                    ins = t_.transpose(ps[:, 6 + k // 4, (k % 4) * P:(k % 4) * P + rows], conv_rows[:, k * P:(k + 1) * P],
                                       ident[0:rows, 0:rows])
                    if k % 4 == 3:
                        ins.then_inc(cc_mm, 1)
                pe.wait_ge(mq_v, 2)
                def taps(ct):
                    pe.wait_ge(gl_v, ct + 1)
                    if ct >= 2:
                        pe.wait_ge(cv_v, ct - 1)
                    for tap in range(PE_TAPS[ct]):
                        k = TAPS_BEFORE[ct] + tap
                        pe.wait_ge(dg_a, k + 1)
                        t_.matmul(ps[:, 6 + ct % 2, :], dg[:, k % DIAGS, :], hpad[:, ct, 2 + tap:2 + tap + S],
                                  start=(tap == 0), stop=(tap == PE_TAPS[ct] - 1)).then_inc(cv_mm, 1)

                for j in range(KD):
                    h = j // 2
                    if j >= 2:
                        pe.wait_ge(gl_v, j - 1)
                    u = UNITS_1 + 2 + 2 * j
                    feature_tile(2 * (j % 2), u).then_inc(units[u][2][0], 1)
                    if j == 0:
                        pe.wait_ge(cc_v, 1)
                    else:
                        taps(j - 1)
                    if j % 2:
                        mem_turn(1, h)
                    else:
                        mem_scores(1, h)
                    feature_tile(2 * (j % 2) + 1, u + 1).then_inc(gate_event(j)[0], 1)
                    if j % 2:
                        mem_weigh(1, h)
                taps(KD - 1)
                for ct in range(KD):
                    pe.wait_ge(cv_v, ct + 1)
                    ins = t_.matmul(ps[:, 0, :], ones[:, :], mixT[:, ct, :], start=(ct == 0), stop=(ct == KD - 1))
                ins.then_inc(mu_mm, 1)
                for ct in range(KD):
                    pe.wait_ge(sq_a, ct + 1)
                    t_.matmul(ps[:, 3, :], ones[:, :], gl[:, ct % 2, :], start=(ct == 0), stop=(ct == KD - 1)).then_inc(var_mm, 1)
                pe.wait_ge(var_v, 1)

            for layer in range(2):
                if layer == 1:
                    pe.wait_ge(xl_v, 2 * 2 * TT)
                    convolution()
                pe.wait_ge(mo_v, MEM_HEADS * (layer + 1))
                out_project(layer)
                route(layer)
                moe(layer)
                if layer == 0:
                    for t in range(TT):
                        x_transpose(2, t)


INPUTS = ["x", "mem", "router_w", "router_bias",
          "l0_w_in", "l0_mem_wkv", "l0_w_o", "l0_ln_g", "l0_ln_b", "l0_moe_w_in", "l0_moe_w_out",
          "l1_w_in", "l1_conv_w", "l1_conv_b", "l1_conv_norm_g", "l1_conv_norm_b", "l1_mem_wkv", "l1_w_o",
          "l1_ln_g", "l1_ln_b", "l1_moe_w_in", "l1_moe_w_out"]


def kernel(**inputs):
    import numpy as _np
    import concourse.bacc as _bacc
    from concourse import mybir as _mybir
    from concourse.bass_utils import run_bass_kernel_spmd as _run

    nc = _bacc.Bacc("TRN2", target_bir_lowering=False, num_devices=1)
    arrays, args = {}, []
    for name in INPUTS:
        a = _np.ascontiguousarray(inputs[name])
        arrays[f"in_{name}"] = a
        args.append(nc.dram_tensor(f"in_{name}", a.shape, _mybir.dt.from_np(a.dtype), kind="ExternalInput").ap())
    out = nc.dram_tensor("out_x", (1, S, D), _mybir.dt.from_np(_np.dtype("float32")), kind="ExternalOutput").ap()
    build(nc, *args, out)
    r = _run(nc, [arrays], core_ids=[0])
    return r.results[0]["out_x"]
```
